# Optimizing a Trainium2 kernel written in Bass

```python
import jax
import jax.numpy as jnp
from jax import lax
import numpy as np

D_MODEL = 1024
BATCH = 1
SEQ = 256
DEPTH = 2

GRID_W = 64
CTX_LEN = 256
HEAD_DIM = 64
ROPE_THETA = 10000.0
EPS = 1e-6
NEG_INF = -1e30
Q_BLOCK = 128
POOL_GROUPS = 4
POOL_GROUP_DIM = 64
POOL_DIM = POOL_GROUPS * POOL_GROUP_DIM
POOL_WINDOWS = (2, 4, 8, 16)
B_Q_HEADS = 12
B_KV_HEADS = 4
D_IN_EVEN = POOL_DIM + (B_Q_HEADS + 2 * B_KV_HEADS) * HEAD_DIM
D_MIX_EVEN = POOL_DIM + B_Q_HEADS * HEAD_DIM
C_Q_HEADS = 16
C_KV_HEADS = 4
WINDOW = 128
D_IN_ODD = (C_Q_HEADS + 2 * C_KV_HEADS) * HEAD_DIM
D_MIX_ODD = C_Q_HEADS * HEAD_DIM
PEER_HEADS = 8
PEER_NKEYS = 128
PEER_N_EXPERTS = PEER_NKEYS * PEER_NKEYS
PEER_DKEY = 256
PEER_TOPK = 16
PEER_CHUNK = 128

N_EVEN = (DEPTH + 1) // 2
N_ODD = DEPTH // 2

kernel_name = "hybrid_pool_gqa_swa_peer_dit"

def rmsnorm(x, g):
    x32 = x.astype(jnp.float32)
    y = x32 * lax.rsqrt(jnp.mean(x32 * x32, axis=-1, keepdims=True) + EPS)
    return (y * g.astype(jnp.float32)).astype(x.dtype)

def modulate(h, shift, scale):
    return h * (1.0 + scale) + shift

def rope_2d_tables(rows):
    row = jnp.repeat(jnp.arange(rows, dtype=jnp.int32), GRID_W).astype(jnp.float32)
    col = jnp.tile(jnp.arange(GRID_W, dtype=jnp.int32), rows).astype(jnp.float32)
    half = HEAD_DIM // 2
    inv = 1.0 / (ROPE_THETA ** (jnp.arange(0, half, 2, dtype=jnp.float32) / half))
    ang_r = row[:, None] * inv[None, :]
    ang_c = col[:, None] * inv[None, :]
    return (jnp.cos(ang_r), jnp.sin(ang_r), jnp.cos(ang_c), jnp.sin(ang_c))

def _rotate(x, cos, sin):
    m = cos.shape[-1]
    x1, x2 = x[..., :m], x[..., m:]
    cs = cos[:, None, :].astype(x.dtype)
    sn = sin[:, None, :].astype(x.dtype)
    return jnp.concatenate([x1 * cs - x2 * sn, x1 * sn + x2 * cs], axis=-1)

def apply_rope_2d(x, rope):
    cr, sr, cc, sc = rope
    h = HEAD_DIM // 2
    return jnp.concatenate([_rotate(x[..., :h], cr, sr), _rotate(x[..., h:], cc, sc)], axis=-1)

def split_gqa(q, n_kv):
    B, L, H, D = q.shape
    return q.reshape(B, L, n_kv, H // n_kv, D)

def softmax_sink(s, sink):
    if sink is None:
        return jax.nn.softmax(s, axis=-1)
    sk = sink.astype(jnp.float32)[None, :, :, None, None]
    m = jnp.maximum(jnp.max(s, axis=-1, keepdims=True), sk)
    e = jnp.exp(s - m)
    return e / (jnp.sum(e, axis=-1, keepdims=True) + jnp.exp(sk - m))

def dense_gqa(q, k, v, sink=None):
    s = jnp.einsum('bqkgd,blkd->bkgql', q, k).astype(jnp.float32) * (HEAD_DIM ** -0.5)
    p = softmax_sink(s, sink)
    return jnp.einsum('bkgql,blkd->bqkgd', p.astype(v.dtype), v)

def global_attn_latent(q_lat, k_all, v_all):
    B, S = q_lat.shape[:2]
    nblk = S // Q_BLOCK
    qb = q_lat.reshape(B, nblk, Q_BLOCK, *q_lat.shape[2:]).swapaxes(0, 1)
    out = lax.map(lambda qi: dense_gqa(qi, k_all, v_all), qb)
    return out.swapaxes(0, 1).reshape(B, S, -1)

def window_attn_latent(q_lat, k_lat, v_lat, k_ctx, v_ctx, sink):
    B, S = q_lat.shape[:2]
    n_ctx = k_ctx.shape[1]
    nblk = S // Q_BLOCK
    band = Q_BLOCK + 2 * WINDOW
    pad = ((0, 0), (WINDOW, WINDOW), (0, 0), (0, 0))
    k_pad = jnp.pad(k_lat, pad)
    v_pad = jnp.pad(v_lat, pad)
    qb = q_lat.reshape(B, nblk, Q_BLOCK, *q_lat.shape[2:]).swapaxes(0, 1)
    scale = HEAD_DIM ** -0.5

    def blk(args):
        i, qi = args
        start = i * Q_BLOCK
        kb = lax.dynamic_slice_in_dim(k_pad, start, band, axis=1)
        vb = lax.dynamic_slice_in_dim(v_pad, start, band, axis=1)
        qpos = start + jnp.arange(Q_BLOCK, dtype=jnp.int32)
        kpos = start - WINDOW + jnp.arange(band, dtype=jnp.int32)
        valid = ((kpos[None, :] >= 0) & (kpos[None, :] < S)
                 & (jnp.abs(qpos[:, None] - kpos[None, :]) <= WINDOW))
        s_band = jnp.einsum('bqkgd,blkd->bkgql', qi, kb).astype(jnp.float32) * scale
        s_band = jnp.where(valid, s_band, NEG_INF)
        s_ctx = jnp.einsum('bqkgd,blkd->bkgql', qi, k_ctx).astype(jnp.float32) * scale
        p = softmax_sink(jnp.concatenate([s_ctx, s_band], axis=-1), sink)
        pc = p[..., :n_ctx].astype(v_ctx.dtype)
        pb = p[..., n_ctx:].astype(vb.dtype)
        return (jnp.einsum('bkgql,blkd->bqkgd', pc, v_ctx)
                + jnp.einsum('bkgql,blkd->bqkgd', pb, vb))

    out = lax.map(blk, (jnp.arange(nblk, dtype=jnp.int32), qb))
    return out.swapaxes(0, 1).reshape(B, S, -1)

def pool_mixer(u, pool_w, pool_scale):
    B, L, _ = u.shape
    ug = u.reshape(B, L, POOL_GROUPS, POOL_GROUP_DIM)
    csum = jnp.pad(jnp.cumsum(ug.astype(jnp.float32), axis=1), ((0, 0), (1, 0), (0, 0), (0, 0)))
    t = jnp.arange(L, dtype=jnp.int32)
    means = []
    for g, w in enumerate(POOL_WINDOWS):
        lo = jnp.clip(t - w // 2, 0, L)
        hi = jnp.clip(t + w - w // 2, 0, L)
        cg = csum[:, :, g]
        ssum = jnp.take(cg, hi, axis=1) - jnp.take(cg, lo, axis=1)
        means.append(ssum / (hi - lo).astype(jnp.float32)[None, :, None])
    pooled = jnp.stack(means, axis=2).astype(u.dtype) - ug
    mixed = jnp.einsum('blgc,gcd->blgd', pooled, pool_w).reshape(B, L, POOL_DIM)
    return mixed * pool_scale

def even_mixer(h_lat, h_ctx, w_in, q_g, k_g, pool_w, pool_scale, w_out, rope, need_ctx):
    splits = [POOL_DIM, POOL_DIM + B_Q_HEADS * HEAD_DIM, POOL_DIM + (B_Q_HEADS + B_KV_HEADS) * HEAD_DIM]

    def project(h):
        B, L, _ = h.shape
        u, q, k, v = jnp.split(h @ w_in, splits, axis=-1)
        q = rmsnorm(q.reshape(B, L, B_Q_HEADS, HEAD_DIM), q_g)
        k = rmsnorm(k.reshape(B, L, B_KV_HEADS, HEAD_DIM), k_g)
        v = v.reshape(B, L, B_KV_HEADS, HEAD_DIM)
        return u, q, k, v

    u_l, q_l, k_l, v_l = project(h_lat)
    u_c, q_c, k_c, v_c = project(h_ctx)
    q_l = apply_rope_2d(q_l, rope)
    k_l = apply_rope_2d(k_l, rope)
    k_all = jnp.concatenate([k_c, k_l], axis=1)
    v_all = jnp.concatenate([v_c, v_l], axis=1)
    a_l = global_attn_latent(split_gqa(q_l, B_KV_HEADS), k_all, v_all)
    y_lat = jnp.concatenate([pool_mixer(u_l, pool_w, pool_scale), a_l], axis=-1) @ w_out
    y_ctx = None
    if need_ctx:
        B, Lc = h_ctx.shape[:2]
        a_c = dense_gqa(split_gqa(q_c, B_KV_HEADS), k_c, v_c).reshape(B, Lc, -1)
        y_ctx = jnp.concatenate([pool_mixer(u_c, pool_w, pool_scale), a_c], axis=-1) @ w_out
    return y_lat, y_ctx

def odd_mixer(h_lat, h_ctx, w_in, sink, w_out, rope, need_ctx):
    splits = [C_Q_HEADS * HEAD_DIM, (C_Q_HEADS + C_KV_HEADS) * HEAD_DIM]

    def project(h):
        B, L, _ = h.shape
        q, k, v = jnp.split(h @ w_in, splits, axis=-1)
        return (q.reshape(B, L, C_Q_HEADS, HEAD_DIM), k.reshape(B, L, C_KV_HEADS, HEAD_DIM),
                v.reshape(B, L, C_KV_HEADS, HEAD_DIM))

    q_l, k_l, v_l = project(h_lat)
    q_c, k_c, v_c = project(h_ctx)
    q_l = apply_rope_2d(q_l, rope)
    k_l = apply_rope_2d(k_l, rope)
    sink_g = sink.reshape(C_KV_HEADS, C_Q_HEADS // C_KV_HEADS)
    a_l = window_attn_latent(split_gqa(q_l, C_KV_HEADS), k_l, v_l, k_c, v_c, sink_g)
    y_lat = a_l @ w_out
    y_ctx = None
    if need_ctx:
        B, Lc = h_ctx.shape[:2]
        y_ctx = dense_gqa(split_gqa(q_c, C_KV_HEADS), k_c, v_c, sink_g).reshape(B, Lc, -1) @ w_out
    return y_lat, y_ctx

def peer(h, w_q, keys1, keys2, u_tab, v_tab):
    T, D = h.shape
    half = PEER_DKEY // 2
    hc = h.reshape(T // PEER_CHUNK, PEER_CHUNK, D)

    def chunk(xc):
        q = (xc @ w_q).reshape(PEER_CHUNK, PEER_HEADS, PEER_DKEY).astype(jnp.float32)
        s1 = jnp.einsum('chd,nd->chn', q[..., :half], keys1.astype(jnp.float32))
        s2 = jnp.einsum('chd,nd->chn', q[..., half:], keys2.astype(jnp.float32))
        v1, i1 = lax.top_k(s1, PEER_TOPK)
        v2, i2 = lax.top_k(s2, PEER_TOPK)
        cand = (v1[..., :, None] + v2[..., None, :]).reshape(PEER_CHUNK, PEER_HEADS, PEER_TOPK * PEER_TOPK)
        sv, si = lax.top_k(cand, PEER_TOPK)
        e1 = jnp.take_along_axis(i1, si // PEER_TOPK, axis=-1)
        e2 = jnp.take_along_axis(i2, si % PEER_TOPK, axis=-1)
        idx = e1 * PEER_NKEYS + e2
        g = jax.nn.softmax(sv, axis=-1)
        u = u_tab[idx]
        a = jax.nn.gelu(jnp.einsum('chkd,cd->chk', u, xc).astype(jnp.float32), approximate=False)
        w = (g * a).astype(xc.dtype)
        return jnp.einsum('chk,chkd->cd', w, v_tab[idx])

    return lax.map(chunk, hc).reshape(T, D)

def setup_inputs(seed: int = 0) -> dict:
    key = jax.random.key(seed)
    ks = jax.random.split(key, 24)
    D = D_MODEL
    nrm = jax.random.normal
    f32 = jnp.float32
    return {
        "x": nrm(ks[0], (BATCH, SEQ, D), f32),
        "c": nrm(ks[1], (BATCH, D), f32),
        "ctx": nrm(ks[2], (BATCH, CTX_LEN, D), f32),
        "c_ctx": nrm(ks[3], (D,), f32),
        "ada_w": nrm(ks[4], (DEPTH, D, 6 * D), f32) * (0.5 * D ** -0.5),
        "ada_b": nrm(ks[5], (DEPTH, 6 * D), f32) * 0.02,
        "norm1_g": 1.0 + 0.05 * nrm(ks[6], (DEPTH, D), f32),
        "norm2_g": 1.0 + 0.05 * nrm(ks[7], (DEPTH, D), f32),
        "final_g": 1.0 + 0.05 * nrm(ks[8], (D,), f32),
        "e_w_in": nrm(ks[9], (N_EVEN, D, D_IN_EVEN), f32) * D ** -0.5,
        "e_q_norm_g": 1.0 + 0.05 * nrm(ks[10], (N_EVEN, HEAD_DIM), f32),
        "e_k_norm_g": 1.0 + 0.05 * nrm(ks[11], (N_EVEN, HEAD_DIM), f32),
        "e_pool_w": nrm(ks[12], (N_EVEN, POOL_GROUPS, POOL_GROUP_DIM, POOL_GROUP_DIM), f32) * POOL_GROUP_DIM ** -0.5,
        "e_pool_scale": 1.0 + 0.1 * nrm(ks[13], (N_EVEN, POOL_DIM), f32),
        "e_w_out": nrm(ks[14], (N_EVEN, D_MIX_EVEN, D), f32) * D_MIX_EVEN ** -0.5,
        "o_w_in": nrm(ks[15], (N_ODD, D, D_IN_ODD), f32) * D ** -0.5,
        "o_sink": nrm(ks[16], (N_ODD, C_Q_HEADS), f32) * 0.5,
        "o_w_out": nrm(ks[17], (N_ODD, D_MIX_ODD, D), f32) * D_MIX_ODD ** -0.5,
        "p_w_q": nrm(ks[18], (DEPTH, D, PEER_HEADS * PEER_DKEY), f32) * D ** -0.5,
        "p_keys1": nrm(ks[19], (DEPTH, PEER_NKEYS, PEER_DKEY // 2), f32) * (PEER_DKEY // 2) ** -0.5,
        "p_keys2": nrm(ks[20], (DEPTH, PEER_NKEYS, PEER_DKEY // 2), f32) * (PEER_DKEY // 2) ** -0.5,
        "p_u": nrm(ks[21], (DEPTH, PEER_N_EXPERTS, D), f32) * D ** -0.5,
        "p_v": nrm(ks[22], (DEPTH, PEER_N_EXPERTS, D), f32),
    }

def reference(x, c, ctx, c_ctx, ada_w, ada_b, norm1_g, norm2_g, final_g,
              e_w_in, e_q_norm_g, e_k_norm_g, e_pool_w, e_pool_scale, e_w_out,
              o_w_in, o_sink, o_w_out,
              p_w_q, p_keys1, p_keys2, p_u, p_v):
    B, S, D = x.shape
    ROWS = S // GRID_W
    rope = rope_2d_tables(ROWS)
    silu_c = jax.nn.silu(c)
    silu_cc = jax.nn.silu(c_ctx)
    for i in range(DEPTH):
        need_ctx = i < DEPTH - 1
        mod = silu_c @ ada_w[i] + ada_b[i]
        mod_c = silu_cc @ ada_w[i] + ada_b[i]
        sh1, sc1, g1, sh2, sc2, g2 = jnp.split(mod[:, None, :], 6, axis=-1)
        csh1, csc1, cg1, csh2, csc2, cg2 = jnp.split(mod_c, 6, axis=-1)

        h_lat = modulate(rmsnorm(x, norm1_g[i]), sh1, sc1)
        h_ctx = modulate(rmsnorm(ctx, norm1_g[i]), csh1, csc1)
        if i % 2 == 0:
            j = i // 2
            y_lat, y_ctx = even_mixer(h_lat, h_ctx, e_w_in[j], e_q_norm_g[j], e_k_norm_g[j],
                                      e_pool_w[j], e_pool_scale[j], e_w_out[j], rope, need_ctx)
        else:
            j = i // 2
            y_lat, y_ctx = odd_mixer(h_lat, h_ctx, o_w_in[j], o_sink[j], o_w_out[j], rope, need_ctx)
        x = x + g1 * y_lat
        h2 = modulate(rmsnorm(x, norm2_g[i]), sh2, sc2)
        if need_ctx:
            ctx = ctx + cg1 * y_ctx
            h2c = modulate(rmsnorm(ctx, norm2_g[i]), csh2, csc2)
            tokens = jnp.concatenate([h2.reshape(-1, D), h2c.reshape(-1, D)], axis=0)
            out = peer(tokens, p_w_q[i], p_keys1[i], p_keys2[i], p_u[i], p_v[i])
            x = x + g2 * out[:B * S].reshape(B, S, D)
            ctx = ctx + cg2 * out[B * S:].reshape(B, -1, D)
        else:
            out = peer(h2.reshape(-1, D), p_w_q[i], p_keys1[i], p_keys2[i], p_u[i], p_v[i])
            x = x + g2 * out.reshape(B, S, D)
    return rmsnorm(x, final_g)


_drawn_inputs = setup_inputs


def setup_inputs(seed=0):
    import zlib

    import numpy as np

    out = dict(_drawn_inputs(seed))
    spreads = {}
    factors = {'e_q_norm_g': 3.848, 'e_k_norm_g': 4.708, 'o_sink': 32.169}
    for name, (base, spread) in spreads.items():
        noise = np.random.default_rng([zlib.crc32(name.encode()), seed]).standard_normal(out[name].shape)
        drawn = base * np.exp(spread * noise) if base else spread * noise
        out[name] = jnp.asarray(drawn.astype(out[name].dtype))
    for name, factor in factors.items():
        out[name] = (out[name] * factor).astype(out[name].dtype)
    return out
```

```python
from contextlib import ExitStack

import concourse.bass as bass
from concourse import mybir

F32 = mybir.dt.float32
U32 = mybir.dt.uint32
I32 = mybir.dt.int32
ALU = mybir.AluOpType
ACT = mybir.ActivationFunctionType
AX = mybir.AxisListType

P = 128
D = 1024
KC = D // P
DEPTH = 2
LAT, CTX = 0, 1
HD = 64
NKV = 4
QH = (12, 16)
QOFF = (256, 0)
KOFF, VOFF, DIN = 1024, 1280, 1536
CW = 256
WSLOTS = 3
EPS = 1e-6
PH = 8
TOPK = 16
NKEYS = 128
NEXP = NKEYS * NKEYS
NU = NV = 8
PAIR = 2 * TOPK
CAND = [(0, 1, 16), (1, 1, 8), (2, 1, 5), (3, 1, 4), (4, 1, 3), (5, 3, 2), (8, 8, 1)]
NCAND = sum(r * c for _, r, c in CAND)
SCALE = HD ** -0.5
LOWEST = -3.0e38
MASKED = -1e30 / SCALE
SH1, SC1, G1, SH2, SC2, G2 = range(6)
HALVES = 12
TILES = ((0, 1, 2, 3), (0, 1))


def schedule():
    s = [("prep",)]
    for l in range(DEPTH):
        streams = (LAT, CTX) if l == 0 else (LAT,)
        s += [("ada", l, k) for k in range(HALVES + 1)]
        s += [("norm", l, 1, st) for st in (LAT, CTX)]
        s += [("hT", l, 1, st) for st in (LAT, CTX)]
        s += [("in", l, b) for b in range(DIN // CW)]
        s += [("rope", l, t) for t in (0, 1, 2, 3) if (l, t) not in ((1, 2), (1, 3))]
        s += [("tqk", l, st) for st in (LAT, CTX)]
        for st in streams:
            s += [("att", l, st)]
            if l == 0:
                s += [("pool", st)]
            s += [("bc", l, st), ("out", l, st), ("norm", l, 2, st), ("hT", l, 2, st)]
        s += [("score", l, LAT, tuple(range(PH))), ("topk", l, 0, 0), ("topk", l, 0, 1)]
        if l == 0:
            after = {(0, 0): [("topk", 0, 1, 0)],
                     (0, 1): [("score", 0, CTX, (0, 1, 2, 3)), ("topk", 0, 1, 1)],
                     (1, 0): [("score", 0, CTX, (4, 5, 6, 7)), ("topk", 0, 2, 0)],
                     (1, 1): [("topk", 0, 2, 1)],
                     (2, 0): [("topk", 0, 3, 0)], (2, 1): [("topk", 0, 3, 1)]}
        else:
            after = {(0, 0): [("topk", 1, 1, 0)], (0, 1): [("topk", 1, 1, 1)]}
        for t in TILES[l]:
            for part in (0, 1):
                s += [("experts", l, t, part)] + after.get((t, part), [])
        s += [("experts_end", l)]
    s += [("final",)]
    return s


SCHEDULE = schedule()


def units(l, st):
    return [(tt, h) for tt in range(2) for h in range(QH[l])]


def score_steps(heads):
    steps = [("Q", heads[0])]
    for i, h in enumerate(heads):
        if i + 1 < len(heads):
            steps.append(("Q", heads[i + 1]))
        steps.append(("R", h))
    return steps


def att_steps(n):
    steps = [("A", 0), ("A", 1)]
    for i in range(n):
        steps.append(("B", i))
        if i + 2 < n:
            steps.append(("A", i + 2))
        steps.append(("C", i))
    return steps


def pool_steps():
    return [("PA", 0), ("PA", 1), ("PB", 0), ("PA", 2), ("PB", 1), ("PA", 3), ("PB", 2), ("PB", 3)]


def in_streams(l, b):
    return (LAT, CTX) if l == 0 or b >= 4 else (LAT,)


def work_order():
    w = []
    for s in SCHEDULE:
        k = s[0]
        if k == "prep":
            w += [(("rows",), "act"), (("keys",), "act")]
        elif k == "ada":
            if s[2] < HALVES:
                w += [(("ada", s[1], s[2]), "act")]
            if s[2] > 0:
                w += [(("adaT", s[1], s[2] - 1), "dve")]
        elif k == "hT":
            w += [(s + (jj,), "act") for jj in range(KC // 2)]
        elif k == "in":
            w += [(s + (st,), "act") for st in in_streams(s[1], s[2])]
        elif k == "tqk":
            nq = QH[s[1]] // 4 if (s[1], s[2]) != (1, CTX) else 0
            w += [(s + ("q", i), "act") for i in range(nq)] + [(s + ("k", i), "act") for i in range(2)]
        elif k == "att":
            w += [(s + (a, i), {"A": "exp", "B": "act", "C": "dve"}[a]) for a, i in att_steps(len(units(s[1], s[2])))]
        elif k == "pool":
            w += [(s + (a, g), "dve") for a, g in pool_steps()]
        elif k == "bc":
            w += [(s + (v, hf), "act") for v in (G1, SC2, SH2, G2) for hf in range(2)]
        elif k == "out":
            w += [(s + (b,), "dve") for b in range(D // CW)]
        elif k == "score":
            w += [(s[:3] + (a, h), "act") for a, h in score_steps(s[3])]
    return w


WORK = work_order()


def block_order():
    o = []
    for s in SCHEDULE:
        if s[0] == "ada" and s[2] < HALVES:
            o += [("ada", s[1], 2 * s[2] + i) for i in range(2)]
        elif s[0] == "in":
            o += [s]
        elif s[0] == "out":
            o += [s + (b,) for b in range(D // CW)]
        elif s[0] == "score":
            o += [("wq", s[1], s[2], h) for h in s[3]]
    return o


BLOCKS = block_order()


class Count:

    def __init__(self, sem, names):
        self.sem, self.pos = sem, {n: i + 1 for i, n in enumerate(names)}

    def at(self, *name):
        return self.pos[name]


def named(*kinds):
    return [s for s in SCHEDULE if s[0] in kinds]


def program(nc, t):
    x_d, c_d, ctx_d, cctx_d = t["x"], t["c"], t["ctx"], t["c_ctx"]
    out_d = t["out"]
    es = ExitStack()
    with es:
        def sb(name, shape, dt=F32):
            return es.enter_context(nc.sbuf_tensor(name, shape, dt))

        def sem(name):
            return es.enter_context(nc.semaphore(name))

        X = sb("X", [P, 4, D])
        H = sb("H", [P, 4, D])
        HT = sb("HT", [P, KC, 4 * P])
        BC = sb("BC", [P, 5, D])
        G1B, A2B, B2B, G2B = BC[:, 0, :], BC[:, 1, :], BC[:, 2, :], (BC[:, 3, :], BC[:, 4, :])
        WR = sb("WR", [P, WSLOTS, KC, CW])
        RING = sb("RING", [P, NU + NV, D])
        U, V = RING[:, 0:NU, :], RING[:, NU:NU + NV, :]
        QKV = RING[:, 0:6, :].rearrange("p a b -> p (a b)").rearrange("p (t n) -> p t n", t=4)
        qT = RING[:, 6:10, :].rearrange("p a b -> p (a b)").rearrange("p (c n) -> p c n", c=8)
        kT = RING[:, 10:12, :].rearrange("p a b -> p (a b)").rearrange("p (c n) -> p c n", c=4)
        YT = [RING[:, 12 + 2 * s:14 + 2 * s, :].rearrange("p a b -> p (a b)").rearrange("p (c n) -> p c n", c=8)
              for s in range(2)]
        SCR = sb("SCR", [P, 4096])
        SC = SCR[:, :].rearrange("p (t s n) -> p t s n", t=2, s=16)
        PR = SCR[:, 0:1024].rearrange("p (r n) -> p r n", r=2)
        PT = SCR[:, 1024:2048].rearrange("p (r n) -> p r n", r=2)
        PM = SCR[:, 2048:4096].rearrange("p (i g n) -> p i g n", i=2, g=4)
        OHR = sb("OHR", [P, 3200])
        OH = OHR[:, :].rearrange("p (h k n) -> p h k n", h=4, k=TOPK)
        T1, T2 = OHR[:, 0:1280], OHR[:, 1280:2560]
        PL = OHR[:, 2560:3072].rearrange("p (r n) -> p r n", r=2)
        R1 = H[0:96, 0, 512:640]
        R2 = H[0:48, 0, 640:768]
        CT = sb("CT", [P, 144])
        KR = H[:, 0, 0:512].rearrange("p (k n) -> p k n", k=4)
        KT = sb("KT", [P, 4, P])
        SIL = sb("SIL", [P, 2, KC])
        SE = sb("SE", [P, 2, KC])
        MOD = sb("MOD", [P, DEPTH, 48, 2])
        MROW = OHR[0:2, 0:1024].rearrange("p (r n) -> p r n", r=2)
        RC = sb("RC", [P, 2, 2, HD])
        GN = sb("GN", [P, 2, HD])
        CG = RING[:, 9, 0:512].rearrange("p (t q c n) -> p t q c n", t=2, q=2, c=2)
        PW = RING[0:HD, 9, 512:768].rearrange("p (g n) -> p g n", g=4)
        SK = sb("SK", [P, 16])
        PS = sb("PS", [P, 2])
        ident = sb("ident", [P, P])
        MK = sb("MK", [P, 2, P])
        EPT = sb("EPT", [P, 1])
        SS = sb("SS", [P, 2])
        RS = sb("RS", [P, 2])
        HS = sb("HS", [P, 16])
        HR = sb("HR", [P, 16])
        STM = sb("STM", [P, 4, 4])
        QS = sb("QS", [P, 2, 2, 2 * P])
        TV = sb("TV", [P, 2, 4, TOPK])
        TI = sb("TI", [P, 2, 4, TOPK], U32)
        TF = sb("TF", [P, 2, 4, TOPK])
        CA = sb("CA", [P, 4, NCAND])
        CI = sb("CI", [P, 4, NCAND])
        SV = sb("SV", [P, 4, TOPK])
        PI = sb("PI", [P, 4, TOPK], U32)
        PF = sb("PF", [P, 4, TOPK])
        IF = sb("IF", [P, 4, TOPK])
        SM = sb("SM", [P, 4])
        IOI = sb("IOI", [P, NCAND], I32)
        IOF = sb("IOF", [P, NCAND])
        IDX = sb("IDX", [P, 4, PH * TOPK], U32)
        WG = sb("WG", [P, 4, PH * TOPK])
        IU = sb("IU", [P, 2, TOPK], U32)
        IV = sb("IV", [P, 2, TOPK], U32)
        A = sb("A", [P, 2, TOPK])
        GA = sb("GA", [P, 2, TOPK])
        WT = sb("WT", [P, 2, TOPK])
        DG = sb("DG", [P, 4, P])
        acc = es.enter_context(nc.psum_tensor("acc", [P, 2, D], F32))
        wk = es.enter_context(nc.psum_tensor("wk", [P, 4, 512], F32))

        loaded = {n: sem("ld_" + n) for n in ("rows", "keys", "x", "ctx", "small", "pm")}
        final_gain = sem("final_gain")
        blk_in = [sem(f"blk{i}") for i in range(WSLOTS)]
        ada_first = sem("ada_first")
        product = sem("product")
        act_evac, dve_evac = sem("act_evac"), sem("dve_evac")
        consts = sem("consts")
        exp_c, silu_done = sem("exp_c"), sem("silu_done")
        norms = [s for s in SCHEDULE if s[0] in ("norm", "final")]
        sumsq = Count(sem("sumsq"), norms)
        sqrted = Count(sem("sqrted"), norms)
        normed = Count(sem("normed"), norms)
        ropes = named("rope")
        hsumsq = Count(sem("hsumsq"), [s for s in ropes if s[1] == 0])
        hsqrt = Count(sem("hsqrt"), [s for s in ropes if s[1] == 0])
        roped = Count(sem("roped"), ropes)
        all_units = [(s[1], s[2], i) for s in named("att") for i in range(len(units(s[1], s[2])))]
        maxed = Count(sem("maxed"), all_units)
        expd = Count(sem("expd"), all_units)
        scaled = Count(sem("scaled"), all_units)
        topks = named("topk")
        shifted = Count(sem("shifted"), topks)
        texp = Count(sem("texp"), topks)
        chosen = Count(sem("chosen"), topks)
        scores_used = Count(sem("scores_used"), topks)
        u_in = [sem(f"u_in{i}") for i in range(NU)]
        v_in = [sem(f"v_in{i}") for i in range(NV)]
        ixcopy, issued, gate_sem = sem("ixcopy"), sem("issued"), sem("gate_sem")
        dotted, gelud, weighted, diag, vsum, updated = (sem(n) for n in (
            "dotted", "gelud", "weighted", "diag", "vsum", "updated"))
        dch, ach = sem("dch"), sem("ach")
        stored = sem("stored")

        work = {n: i for i, (n, _) in enumerate(WORK)}

        def evac(name):
            i = work[name]
            e = WORK[i][1]
            if e == "exp":
                return expd.sem, expd.at(name[1], name[2], name[4])
            return (act_evac if e == "act" else dve_evac), sum(1 for _, x in WORK[:i + 1] if x == e)

        def bank(name):
            return wk[:, work[name] % 4, :]

        blk = {n: i for i, n in enumerate(BLOCKS)}

        def block_used(name):
            kind, l, b = name[0], name[1], name[-1]
            if kind == "ada" and b % 2 == 0:
                return ada_first, HALVES * l + b // 2 + 1
            last = {"ada": ("ada", l, b // 2), "in": name + (in_streams(l, b)[-1],), "out": name,
                    "wq": ("score",) + name[1:3] + ("Q", b)}[kind]
            return product, work[last] + 1

        def chunk0(l, t):
            return 32 * l + PH * t

        block = es.enter_context(nc.Block())

        @block.sync
        def _(sp):
            rows = [(R1[0:8], c_d.rearrange("o (j p) -> (o j) p", p=P)),
                    (R1[8:16], cctx_d.rearrange("(j p) -> j p", p=P)),
                    (R1[16:32], t["norm1_g"].rearrange("l (j p) -> (l j) p", p=P)),
                    (R1[32:48], t["norm2_g"].rearrange("l (j p) -> (l j) p", p=P)),
                    (R1[48:96], t["ada_b"][0].rearrange("(j p) -> j p", p=P)),
                    (R2[:, :], t["ada_b"][1].rearrange("(j p) -> j p", p=P))]
            for dst, src in rows:
                sp.dma_start(dst, src).then_inc(loaded["rows"], 16)
            for l in range(DEPTH):
                sp.dma_start(KR[:, 2 * l, :], t["p_keys1"][l]).then_inc(loaded["keys"], 16)
                sp.dma_start(KR[:, 2 * l + 1, :], t["p_keys2"][l]).then_inc(loaded["keys"], 16)
            srcs = {"ada": t["ada_w"], "out": (t["e_w_out"], t["o_w_out"]), "in": (t["e_w_in"], t["o_w_in"]),
                    "wq": t["p_w_q"]}
            for i, name in enumerate(BLOCKS):
                if i == 2:
                    sp.dma_start(X[:, 0:2, :], x_d[0].rearrange("(a p) d -> p a d", p=P)).then_inc(loaded["x"], 16)
                    sp.dma_start(X[:, 2:4, :], ctx_d[0].rearrange("(a p) d -> p a d", p=P)).then_inc(loaded["ctx"], 16)
                if i == 4:
                    sp.dma_start(RC[:, :, :, :], t["rope"]).then_inc(loaded["small"], 16)
                    sp.dma_start(GN[:, 0, :], t["e_q_norm_g"].partition_broadcast(P)[:, 0, :]).then_inc(loaded["small"], 16)
                    sp.dma_start(GN[:, 1, :], t["e_k_norm_g"].partition_broadcast(P)[:, 0, :]).then_inc(loaded["small"], 16)
                    sp.dma_start(SK[:, :], t["o_sink"].partition_broadcast(P)[:, 0, :]).then_inc(loaded["small"], 16)
                    sp.dma_start(PW[:, :, :], t["e_pool_w"][0].rearrange("g c d -> c g d")).then_inc(loaded["small"], 16)
                    with nc.allow_non_contiguous_dma(reason="256 words"):
                        sp.dma_start(PS[:, :], t["e_pool_scale"][0].rearrange("(j p) -> p j", p=P)).then_inc(loaded["small"], 16)
                    sp.dma_start(PM[:, :, :, :], t["pool_m"]).then_inc(loaded["pm"], 16)
                if i >= WSLOTS:
                    sp.wait_ge(*block_used(BLOCKS[i - WSLOTS]))
                kind, l, b = name[0], name[1], name[-1]
                w = srcs[kind][0] if (kind in ("in", "out") and l == 0) else \
                    srcs[kind][1] if kind in ("in", "out") else srcs[kind][l]
                if kind in ("in", "out"):
                    w = w[0]
                sp.dma_start(WR[:, i % WSLOTS, :, :],
                             w.rearrange("(j p) n -> p j n", p=P)[:, :, b * CW:(b + 1) * CW]).then_inc(blk_in[i % WSLOTS], 16)
            sp.wait_ge(normed.sem, normed.at("norm", 1, 2, LAT))
            sp.wait_ge(*evac(("out", 1, LAT, D // CW - 1)))
            sp.dma_start(G1B, t["final_g"].partition_broadcast(P)).then_inc(final_gain, 16)
            sp.wait_ge(normed.sem, normed.at("final"))
            sp.dma_start(out_d[0].rearrange("(a p) d -> p a d", p=P), H[:, 0:2, :]).then_inc(stored, 16)
            sp.wait_ge(stored, 16)

        @block.gpsimd
        def _(pool):
            nc.gpsimd.memset(ident[:, :], 0.0).then_inc(consts, 1)
            nc.gpsimd.memset(MK[:, :, :], 0.0).then_inc(consts, 1)
            pool.wait_ge(consts, 2)
            nc.gpsimd.affine_select(out=ident[:, :], in_=ident[:, :], compare_op=ALU.not_equal, fill=1.0,
                                    base=0, pattern=[[-1, P]], channel_multiplier=1).then_inc(consts, 1)
            nc.gpsimd.affine_select(out=MK[:, 0, :], in_=MK[:, 0, :], compare_op=ALU.is_ge, fill=MASKED,
                                    base=0, pattern=[[-1, P]], channel_multiplier=1).then_inc(consts, 1)
            nc.gpsimd.affine_select(out=MK[:, 1, :], in_=MK[:, 1, :], compare_op=ALU.is_ge, fill=MASKED,
                                    base=0, pattern=[[1, P]], channel_multiplier=-1).then_inc(consts, 1)
            nc.gpsimd.iota(IOI[:, :], pattern=[[1, NCAND]], base=0, channel_multiplier=0).then_inc(consts, 1)
            tables = {"u": t["p_u"].rearrange("l n d -> (l n) d"), "v": t["p_v"].rearrange("l n d -> (l n) d")}

            def gate(s, value):
                pool.wait_ge(s, value)
                pool.sem_inc(gate_sem, 1)

            def copy_rows(dst, tile, col):
                nc.gpsimd.tensor_copy(dst, IDX[:, tile, col]).then_inc(ixcopy, 1)

            def gather(table, ring, n, rows, slot_in):
                pool.indirect_dma_start(out=ring[:, n % NU, :], out_offset=None, in_=tables[table],
                                        in_offset=bass.IndirectOffsetOnAxis(ap=rows, axis=0),
                                        engine_sem=issued).then_inc(slot_in[n % NU], 16)

            def chunk(l, tile, p, hh, vtile, vcol, first):
                c = chunk0(l, tile) + 2 * p + hh
                start = first and hh == 0 and tile == 0
                static = isinstance(p, int)
                if not (static and c < 2):
                    (gate)(issued, 32 * c - 48)
                col = (2 * p + hh) * TOPK
                copy_rows(IU[:, hh, :], tile, slice(col, col + TOPK) if static else bass.ds(col, TOPK))
                if not start:
                    copy_rows(IV[:, 1 - hh, :], vtile, vcol)
                gate(ixcopy, 2 * c + 1)
                for s in range(TOPK):
                    if not (static and c == 0 and s < NU):
                        gate(dotted, c * TOPK + s - NU + 1)
                    gather("u", U, s, IU[:, hh, s:s + 1], u_in)
                    if not start:
                        if not (static and c == 1 and s < NV):
                            gate(vsum, (c - 1) * TOPK + s - NV + 1)
                        gather("v", V, s, IV[:, 1 - hh, s:s + 1], v_in)

            for s in SCHEDULE:
                if s[0] == "experts":
                    _, l, tile, part = s
                    if part == 0:
                        pool.wait_ge(chosen.sem, chosen.at("topk", l, tile, 0))
                        last = slice(7 * TOPK, 8 * TOPK)
                        chunk(l, tile, 0, 0, tile - 1, last, True)
                        chunk(l, tile, 0, 1, tile, slice(0, TOPK), False)
                    else:
                        pool.wait_ge(chosen.sem, chosen.at("topk", l, tile, 1))
                        with pool.Fori(1, PH // 2) as p:
                            chunk(l, tile, p, 0, tile, bass.ds((2 * p - 1) * TOPK, TOPK), False)
                            chunk(l, tile, p, 1, tile, bass.ds(2 * p * TOPK, TOPK), False)
                elif s[0] == "experts_end":
                    l = s[1]
                    tile = TILES[l][-1]
                    c = chunk0(l, tile) + PH
                    pool.wait_ge(issued, 32 * c - 48)
                    copy_rows(IV[:, 1, :], tile, slice(7 * TOPK, 8 * TOPK))
                    pool.wait_ge(ixcopy, 2 * c)
                    for s_ in range(TOPK):
                        pool.wait_ge(vsum, (c - 1) * TOPK + s_ - NV + 1)
                        gather("v", V, s_, IV[:, 1, s_:s_ + 1], v_in)

        @block.vector
        def _(dve):
            last = [None, 0]

            def op(ins, s=None, value=None):
                if s is None:
                    last[1] += 1
                    ins.then_inc(dch, 1)
                    last[0] = (dch, last[1])
                else:
                    ins.then_inc(s, 1)
                    last[0] = (s, value)

            def after():
                dve.wait_ge(*last[0])

            def taken(ins, name):
                op(ins, *evac(name))

            def ready(name):
                dve.wait_ge(product, work[name] + 1)

            def topk16(vals, idxs, rows):
                op(nc.vector.max(out=vals[:, 0:8], in_=rows))
                after()
                op(nc.vector.max_index(out=idxs[:, 0:8], in_max=vals[:, 0:8], in_values=rows))
                after()
                op(nc.vector.match_replace(out=rows, in_to_replace=vals[:, 0:8], in_values=rows, imm_value=LOWEST))
                after()
                op(nc.vector.max(out=vals[:, 8:16], in_=rows))
                after()
                op(nc.vector.max_index(out=idxs[:, 8:16], in_max=vals[:, 8:16], in_values=rows))

            def dots(c, hh, tile):
                for s in range(TOPK):
                    dve.wait_ge(u_in[s % NU], 16 * (2 * c + s // NU + 1))
                    nc.vector.scalar_tensor_tensor(out=U[:, s % NU, :], in0=U[:, s % NU, :], scalar=1.0,
                                                   in1=H[:, tile, :], op0=ALU.mult, op1=ALU.mult,
                                                   accum_out=A[:, hh, s:s + 1]).then_inc(dotted, 1)

            def update(c, par, tile):
                g2 = G2B[tile // 2]
                dve.wait_ge(vsum, (c + 1) * TOPK)
                nc.vector.tensor_tensor(acc[:, par, :], acc[:, par, :], g2, ALU.mult).then_inc(updated, 1)
                dve.wait_ge(updated, 2 * c + 1)
                nc.vector.tensor_tensor(X[:, tile, :], X[:, tile, :], acc[:, par, :], ALU.add).then_inc(updated, 1)

            def chunk(l, tile, p, hh, vtile, start):
                c = chunk0(l, tile) + 2 * p + hh
                dots(c, hh, tile)
                dve.wait_ge(gelud, c + 1)
                col = (2 * p + hh) * TOPK
                g = WG[:, tile, col:col + TOPK] if isinstance(p, int) else WG[:, tile, bass.ds(col, TOPK)]
                nc.vector.tensor_tensor(WT[:, hh, :], GA[:, hh, :], g, ALU.mult).then_inc(weighted, 1)
                if not start:
                    update(c - 1, 1 - hh, vtile)

            for s in SCHEDULE:
                kind = s[0]
                if kind == "prep":
                    op(nc.vector.memset(EPT[:, :], EPS))
                    dve.wait_ge(consts, 6)
                    op(nc.vector.tensor_copy(IOF[:, :], IOI[:, :]))
                    dve.wait_ge(exp_c, 1)
                    op(nc.vector.tensor_scalar_add(SE[:, :, :], SE[:, :, :], 1.0))
                    after()
                    op(nc.vector.reciprocal(SE[:, :, :], SE[:, :, :]))
                    after()
                    op(nc.vector.tensor_tensor(SIL[:, :, :], SE[:, :, :],
                                               CT[:, 0:16].rearrange("p (s j) -> p s j", s=2), ALU.mult), silu_done, 1)
                    dve.wait_ge(loaded["small"], 96)
                    for tt in range(2):
                        cosb = RC[:, tt, 0, :].unsqueeze(1).to_broadcast([P, 2, HD])
                        op(nc.vector.tensor_tensor(CG[:, tt, :, 0, :], GN[:, :, :], cosb, ALU.mult))
                        for a in range(2):
                            for q in range(2):
                                o = CG[:, tt, q, 1, :].rearrange("p (h a n) -> p h a n", h=2, a=2)[:, :, a, :]
                                sn = RC[:, tt, 1, :].rearrange("p (h a n) -> p h a n", h=2, a=2)[:, :, a, :]
                                g = GN[:, q, :].rearrange("p (h a n) -> p h a n", h=2, a=2)[:, :, 1 - a, :]
                                op(nc.vector.tensor_tensor(o, sn, g, ALU.mult))
                elif kind == "ada" and s[2] > 0:
                    l, k = s[1], s[2] - 1
                    name = ("adaT", l, k)
                    ready(name)
                    cols = MOD[:, l, 4 * k:4 * k + 4, :]
                    bias = CT[:, 48 + 48 * l + 4 * k:48 + 48 * l + 4 * k + 4].unsqueeze(2).to_broadcast([P, 4, 2])
                    add = nc.vector.tensor_tensor(cols, bank(name)[:, 0:8].rearrange("p (k s) -> p k s", s=2), bias, ALU.add)
                    if k // 2 in (SC1, SC2):
                        op(add)
                        after()
                        g0 = (16 if k // 2 == SC1 else 32) + 8 * l + 4 * (k % 2)
                        gain = CT[:, g0:g0 + 4].unsqueeze(2).to_broadcast([P, 4, 2])
                        taken(nc.vector.scalar_tensor_tensor(out=cols, in0=cols, scalar=1.0, in1=gain,
                                                             op0=ALU.add, op1=ALU.mult), name)
                    else:
                        taken(add, name)
                elif kind in ("norm", "final"):
                    st = s[3] if kind == "norm" else LAT
                    if s == ("norm", 0, 1, LAT):
                        dve.wait_ge(loaded["x"], 16)
                        dve.wait_ge(*evac(("keys",)))
                    if s == ("norm", 0, 1, CTX):
                        dve.wait_ge(loaded["ctx"], 16)
                    if last[0] is not None:
                        after()
                    for tt in range(2):
                        ins = nc.vector.scalar_tensor_tensor(
                            out=H[:, 2 * st + tt, :], in0=X[:, 2 * st + tt, :], scalar=1.0, in1=X[:, 2 * st + tt, :],
                            op0=ALU.mult, op1=ALU.mult, accum_out=SS[:, tt:tt + 1])
                        if tt == 0:
                            op(ins)
                    op(ins, sumsq.sem, sumsq.at(*s))
                    dve.wait_ge(sqrted.sem, sqrted.at(*s))
                    op(nc.vector.reciprocal(RS[:, :], SS[:, :]))
                    after()
                    if kind == "norm" and s[2] == 2:
                        dve.wait_ge(*evac(("bc", s[1], st, SH2, 1)))
                    if kind == "final":
                        dve.wait_ge(final_gain, 16)
                    for tt in range(2):
                        h, x, r = H[:, 2 * st + tt, :], X[:, 2 * st + tt, :], RS[:, tt:tt + 1]
                        if kind == "norm" and s[2] == 1:
                            ins = nc.vector.tensor_scalar(h, x, r, None, ALU.mult)
                        elif kind == "final":
                            ins = nc.vector.scalar_tensor_tensor(out=h, in0=x, scalar=r, in1=G1B, op0=ALU.mult, op1=ALU.mult)
                        else:
                            op(nc.vector.scalar_tensor_tensor(out=h, in0=x, scalar=r, in1=A2B, op0=ALU.mult, op1=ALU.mult))
                            after()
                            ins = nc.vector.tensor_tensor(h, h, B2B, ALU.add)
                        if tt == 0:
                            op(ins)
                    op(ins, normed.sem, normed.at(*s))
                elif kind == "rope":
                    l, tile = s[1], s[2]
                    st, tt = tile // 2, tile % 2
                    dve.wait_ge(*evac(("in", l, 5, st)))
                    after()
                    nh = 16 if l == 0 else 20
                    R = QKV[:, tile, QOFF[l]:QOFF[l] + nh * HD].rearrange("p (h n) -> p h n", n=HD)
                    a1 = T1[:, 0:nh * HD].rearrange("p (h n) -> p h n", n=HD)
                    a2 = T2[:, 0:nh * HD].rearrange("p (h n) -> p h n", n=HD)
                    if l == 0:
                        op(nc.vector.tensor_tensor(a1, R, R, ALU.mult))
                        after()
                        op(nc.vector.tensor_reduce(out=HS[:, :], in_=a1, axis=AX.X, op=ALU.add), hsumsq.sem, hsumsq.at(*s))
                        dve.wait_ge(hsqrt.sem, hsqrt.at(*s))
                        op(nc.vector.reciprocal(HR[:, :], HS[:, :]))
                        after()
                        op(nc.vector.tensor_tensor(R, R, HR[:, :].unsqueeze(2).to_broadcast([P, nh, HD]), ALU.mult))
                        after()
                        groups = [(0, 12, 0), (12, 16, 1)]
                    else:
                        groups = [(0, 20, None)]
                    if st == CTX:
                        for lo, hi, q in groups:
                            ins = nc.vector.tensor_tensor(
                                R[:, lo:hi, :], R[:, lo:hi, :],
                                GN[:, q, :].unsqueeze(1).to_broadcast([P, hi - lo, HD]), ALU.mult)
                            if lo == 0:
                                op(ins)
                        op(ins, roped.sem, roped.at(*s))
                    else:
                        for lo, hi, q in groups:
                            tab = RC[:, tt, :, :] if q is None else CG[:, tt, q, :, :]
                            op(nc.vector.tensor_tensor(a1[:, lo:hi, :], R[:, lo:hi, :],
                                                       tab[:, 0, :].unsqueeze(1).to_broadcast([P, hi - lo, HD]), ALU.mult))
                            for a in range(2):
                                for half in range(2):
                                    o = 32 * half + 16 * a
                                    i = 32 * half + 16 * (1 - a)
                                    op(nc.vector.tensor_tensor(
                                        a2[:, lo:hi, o:o + 16], R[:, lo:hi, i:i + 16],
                                        tab[:, 1, o:o + 16].unsqueeze(1).to_broadcast([P, hi - lo, 16]), ALU.mult))
                        after()
                        op(nc.vector.tensor_tensor(R, a1, a2, ALU.add), roped.sem, roped.at(*s))
                elif kind == "att":
                    _, l, st = s
                    us = units(l, st)
                    n = len(us)
                    nk = 512 if st == LAT else 256

                    def rowmax(i):
                        name = s + ("A", i)
                        tt, h = us[i]
                        ready(name)
                        op(nc.vector.reduce_max(STM[:, i % 4, 0:1], bank(name)[:, 0:nk], AX.X))
                        after()
                        if l == 0:
                            op(nc.vector.tensor_scalar(STM[:, i % 4, 1:2], STM[:, i % 4, 0:1], -SCALE, None, ALU.mult),
                               maxed.sem, maxed.at(l, st, i))
                        else:
                            op(nc.vector.tensor_scalar(STM[:, i % 4, 1:2], STM[:, i % 4, 0:1], SCALE, SK[:, h:h + 1],
                                                       ALU.mult, ALU.max))
                            after()
                            op(nc.vector.tensor_scalar(STM[:, i % 4, 1:2], STM[:, i % 4, 1:2], -1.0, None, ALU.mult),
                               maxed.sem, maxed.at(l, st, i))

                    def rescale(i):
                        dve.wait_ge(expd.sem, expd.at(l, st, i))
                        if l == 1:
                            op(nc.vector.tensor_tensor(STM[:, i % 4, 2:3], STM[:, i % 4, 2:3], STM[:, i % 4, 3:4], ALU.add))
                            after()
                        op(nc.vector.reciprocal(STM[:, i % 4, 2:3], STM[:, i % 4, 2:3]))
                        after()
                        op(nc.vector.tensor_scalar(PR[:, i % 2, 0:nk], PR[:, i % 2, 0:nk], STM[:, i % 4, 2:3], None, ALU.mult),
                           scaled.sem, scaled.at(l, st, i))

                    rowmax(0)
                    rowmax(1)
                    rescale(0)
                    for i, (tt, h) in enumerate(us):
                        if i + 1 < n:
                            rescale(i + 1)
                        if i + 2 < n:
                            rowmax(i + 2)
                        name = s + ("C", i)
                        ready(name)
                        o = 64 * (h % 2)
                        c = (2 if l == 0 else 0) + h // 2
                        taken(nc.vector.tensor_copy(YT[st][o:o + 64, c, tt * P:tt * P + P], bank(name)[o:o + 64, 0:P]), name)
                elif kind == "pool":
                    st = s[1]
                    for a, g in pool_steps():
                        name = s + (a, g)
                        ready(name)
                        if a == "PA":
                            taken(nc.vector.tensor_copy(PL[0:64, g % 2, :], bank(name)[0:64, 0:256]), name)
                        else:
                            o = 64 * (g % 2)
                            taken(nc.vector.tensor_scalar(YT[st][o:o + 64, g // 2, :], bank(name)[o:o + 64, 0:256],
                                                          PS[o:o + 64, g // 2:g // 2 + 1], None, ALU.mult), name)
                elif kind == "out":
                    _, l, st = s
                    dve.wait_ge(*evac(("bc", l, st, G1, 1)))
                    for b in range(D // CW):
                        name = s + (b,)
                        ready(name)
                        y = bank(name).rearrange("p (a n) -> p a n", a=2)
                        g = G1B[:, b * CW:(b + 1) * CW].unsqueeze(1).to_broadcast([P, 2, CW])
                        x = X[:, 2 * st:2 * st + 2, b * CW:(b + 1) * CW]
                        op(nc.vector.tensor_tensor(y, y, g, ALU.mult))
                        after()
                        taken(nc.vector.tensor_tensor(x, x, y, ALU.add), name)
                elif kind == "topk":
                    _, l, tile, hf = s
                    st, tt = tile // 2, tile % 2
                    after()
                    for h in range(4):
                        dve.wait_ge(*evac(("score", l, st, "R", 4 * hf + h)))
                        for side in range(2):
                            topk16(TV[:, side, h, :], TI[:, side, h, :], SC[:, tt, 2 * (4 * hf + h) + side, :])
                    after()
                    op(nc.vector.tensor_scalar(TF[:, 0, :, :], TI[:, 0, :, :], float(NKEYS), float(l * NEXP), ALU.mult, ALU.add),
                       scores_used.sem, scores_used.at(*s))
                    op(nc.vector.tensor_copy(TF[:, 1, :, :], TI[:, 1, :, :]))
                    after()
                    for dst, src in ((CA, TV), (CI, TF)):
                        o = 0
                        for r0, nr, ncol in CAND:
                            out = dst[:, :, o:o + nr * ncol].rearrange("p h (a b) -> p h a b", a=nr)
                            first = src[:, 0, :, r0:r0 + nr].unsqueeze(3).to_broadcast([P, 4, nr, ncol])
                            second = src[:, 1, :, 0:ncol].unsqueeze(2).to_broadcast([P, 4, nr, ncol])
                            op(nc.vector.tensor_tensor(out, first, second, ALU.add))
                            o += nr * ncol
                    after()
                    for h in range(4):
                        topk16(SV[:, h, :], PI[:, h, :], CA[:, h, :])
                    after()
                    op(nc.vector.tensor_copy(SM[:, :], SV[:, :, 0]))
                    after()
                    op(nc.vector.tensor_tensor(SV[:, :, :], SV[:, :, :], SM[:, :].unsqueeze(2).to_broadcast([P, 4, TOPK]), ALU.subtract),
                       shifted.sem, shifted.at(*s))
                    op(nc.vector.tensor_copy(PF[:, :, :], PI[:, :, :]))
                    after()
                    k50 = [P, 4 * TOPK, NCAND]
                    oh3 = OHR[:, :].rearrange("p (k n) -> p k n", n=NCAND)
                    op(nc.vector.tensor_tensor(oh3, PF[:, :, :].rearrange("p h k -> p (h k)").unsqueeze(2).to_broadcast(k50),
                                               IOF[:, :].unsqueeze(1).to_broadcast(k50), ALU.is_equal))
                    after()
                    op(nc.vector.tensor_tensor(OH, OH, CI[:, :, :].unsqueeze(2).to_broadcast([P, 4, TOPK, NCAND]), ALU.mult))
                    after()
                    op(nc.vector.tensor_reduce(out=IF[:, :, :].rearrange("p h k -> p (h k)"), in_=oh3, axis=AX.X, op=ALU.add))
                    after()
                    cols = slice(64 * hf, 64 * hf + 64)
                    op(nc.vector.tensor_copy(IDX[:, tile, cols], IF[:, :, :].rearrange("p h k -> p (h k)")))
                    dve.wait_ge(texp.sem, texp.at(*s))
                    op(nc.vector.tensor_reduce(out=SM[:, :], in_=SV[:, :, :], axis=AX.X, op=ALU.add))
                    after()
                    op(nc.vector.reciprocal(SM[:, :], SM[:, :]))
                    after()
                    op(nc.vector.tensor_tensor(WG[:, tile, cols].rearrange("p (h k) -> p h k", k=TOPK), SV[:, :, :],
                                               SM[:, :].unsqueeze(2).to_broadcast([P, 4, TOPK]), ALU.mult),
                       chosen.sem, chosen.at(*s))
                elif kind == "experts":
                    _, l, tile, part = s
                    if part == 0:
                        after()
                        chunk(l, tile, 0, 0, tile - 1, tile == 0)
                        chunk(l, tile, 0, 1, tile, False)
                        last[0] = (updated, 2 * chunk0(l, tile) + 2)
                    else:
                        with dve.Fori(1, PH // 2) as p:
                            chunk(l, tile, p, 0, tile, False)
                            chunk(l, tile, p, 1, tile, False)
                        last[0] = (updated, 2 * (chunk0(l, tile) + PH - 1))
                elif kind == "experts_end":
                    l = s[1]
                    tile = TILES[l][-1]
                    c = chunk0(l, tile) + PH - 1
                    update(c, 1, tile)
                    last[0] = (updated, 2 * c + 2)

        @block.scalar
        def _(act):
            def taken(ins, name):
                ins.then_inc(act_evac, 1)

            def ready(name):
                act.wait_ge(product, work[name] + 1)

            def gelu(c, hh):
                act.wait_ge(dotted, (c + 1) * TOPK)
                nc.scalar.activation(GA[:, hh, :], A[:, hh, :], ACT.Gelu).then_inc(gelud, 1)

            def diags(c, hh):
                act.wait_ge(weighted, c + 1)
                for s in range(TOPK):
                    if not (isinstance(c, int) and c == 0 and s < 4):
                        act.wait_ge(vsum, c * TOPK + s - 3)
                    nc.scalar.activation(DG[:, s % 4, :], ident[:, :], ACT.Copy, scale=WT[:, hh, s:s + 1]).then_inc(diag, 1)

            for s in SCHEDULE:
                kind = s[0]
                if kind == "prep":
                    ready(("rows",))
                    taken(nc.scalar.activation(CT[:, :], bank(("rows",))[:, 0:144], ACT.Copy), ("rows",))
                    act.wait_ge(act_evac, 1)
                    nc.scalar.activation(SE[:, :, :], CT[:, 0:16].rearrange("p (s j) -> p s j", s=2), ACT.Exp,
                                         scale=-1.0).then_inc(exp_c, 1)
                    ready(("keys",))
                    taken(nc.scalar.activation(KT[:, :, :].rearrange("p k n -> p (k n)"), bank(("keys",)), ACT.Copy), ("keys",))
                elif kind == "ada" and s[2] < HALVES:
                    ready(s)
                    taken(nc.scalar.activation(MROW[:, s[2] % 2, :], bank(s)[0:2, :], ACT.Copy), s)
                elif kind in ("norm", "final"):
                    act.wait_ge(sumsq.sem, sumsq.at(*s))
                    nc.scalar.activation(SS[:, :], SS[:, :], ACT.Sqrt, bias=EPT[:, :], scale=1.0 / D).then_inc(sqrted.sem, 1)
                elif kind == "hT":
                    _, l, which, st = s
                    if which == 1:
                        act.wait_ge(*evac(("adaT", l, 3)))
                    for jj in range(KC // 2):
                        name = s + (jj,)
                        ready(name)
                        cols = slice(st * 256, st * 256 + 256)
                        if which == 1:
                            for c in range(2):
                                j = 2 * jj + c
                                ins = nc.scalar.activation(HT[:, j, cols], bank(name)[:, c * 256:c * 256 + 256], ACT.Identity,
                                                           bias=MOD[:, l, SH1 * 8 + j, st:st + 1],
                                                           scale=MOD[:, l, SC1 * 8 + j, st:st + 1])
                        else:
                            ins = nc.scalar.activation(HT[:, 2 * jj:2 * jj + 2, cols],
                                                       bank(name).rearrange("p (c n) -> p c n", c=2), ACT.Copy)
                        taken(ins, name)
                elif kind == "in":
                    _, l, b = s
                    for st in in_streams(l, b):
                        name = s + (st,)
                        ready(name)
                        taken(nc.scalar.activation(QKV[:, 2 * st:2 * st + 2, b * CW:(b + 1) * CW],
                                                   bank(name).rearrange("p (a n) -> p a n", a=2), ACT.Copy), name)
                elif kind == "rope" and s[1] == 0:
                    act.wait_ge(hsumsq.sem, hsumsq.at(*s))
                    nc.scalar.activation(HS[:, :], HS[:, :], ACT.Sqrt, bias=EPT[:, :], scale=1.0 / HD).then_inc(hsqrt.sem, 1)
                elif kind == "tqk":
                    _, l, st = s
                    cols = slice(st * 256, st * 256 + 256)
                    for name, _ in WORK:
                        if name[:3] == s:
                            ready(name)
                            dst = qT if name[3] == "q" else kT
                            i = name[4]
                            taken(nc.scalar.activation(dst[:, 2 * i:2 * i + 2, cols],
                                                       bank(name).rearrange("p (c n) -> p c n", c=2), ACT.Copy), name)
                elif kind == "att":
                    _, l, st = s
                    us = units(l, st)
                    n = len(us)
                    nk = 512 if st == LAT else 256

                    def exps(i):
                        name = s + ("A", i)
                        ready(name)
                        act.wait_ge(maxed.sem, maxed.at(l, st, i))
                        if l == 1:
                            h = us[i][1]
                            nc.scalar.activation(STM[:, i % 4, 3:4], SK[:, h:h + 1], ACT.Exp,
                                                 bias=STM[:, i % 4, 1:2]).then_inc(ach, 1)
                        nc.scalar.activation(PR[:, i % 2, 0:nk], bank(name)[:, 0:nk], ACT.Exp, bias=STM[:, i % 4, 1:2],
                                             scale=SCALE, accum_out=STM[:, i % 4, 2:3]).then_inc(expd.sem, 1)

                    exps(0)
                    exps(1)
                    for i in range(n):
                        name = s + ("B", i)
                        ready(name)
                        taken(nc.scalar.activation(PT[:, i % 2, 0:nk], bank(name)[:, 0:nk], ACT.Copy), name)
                        if i + 2 < n:
                            exps(i + 2)
                elif kind == "bc":
                    _, l, st = s
                    if s != ("bc", 0, LAT):
                        prev = ("norm", 0, 2, LAT if l == 0 else CTX)
                        act.wait_ge(normed.sem, normed.at(*prev))
                    for v, dst in ((G1, G1B), (SC2, A2B), (SH2, B2B), (G2, G2B[st])):
                        for hf in range(2):
                            name = s + (v, hf)
                            ready(name)
                            taken(nc.scalar.activation(dst[:, hf * 512:hf * 512 + 512], bank(name), ACT.Copy), name)
                elif kind == "score":
                    _, l, st, heads = s
                    for a, h in score_steps(heads):
                        name = ("score", l, st, a, h)
                        ready(name)
                        if a == "Q":
                            taken(nc.scalar.activation(QS[:, h % 2, :, :], bank(name).rearrange("p (a n) -> p a n", a=2),
                                                       ACT.Copy), name)
                        else:
                            if st == CTX:
                                act.wait_ge(scores_used.sem, scores_used.at("topk", l, 1, h // 4))
                            taken(nc.scalar.activation(SC[:, :, 2 * h:2 * h + 2, :],
                                                       bank(name).rearrange("p (a s n) -> p a s n", a=2, s=2), ACT.Copy), name)
                elif kind == "topk":
                    act.wait_ge(shifted.sem, shifted.at(*s))
                    nc.scalar.activation(SV[:, :, :], SV[:, :, :], ACT.Exp).then_inc(texp.sem, 1)
                elif kind == "experts":
                    _, l, tile, part = s
                    c0 = chunk0(l, tile)
                    if part == 0:
                        if tile > 0:
                            diags(c0 - 1, 1)
                        gelu(c0, 0)
                        diags(c0, 0)
                        gelu(c0 + 1, 1)
                    else:
                        with act.Fori(1, PH // 2) as p:
                            diags(c0 + 2 * p - 1, 1)
                            gelu(c0 + 2 * p, 0)
                            diags(c0 + 2 * p, 0)
                            gelu(c0 + 2 * p + 1, 1)
                elif kind == "experts_end":
                    diags(chunk0(s[1], TILES[s[1]][-1]) + PH - 1, 1)

        @block.tensor
        def _(pe):
            n_work = [0]

            def begin(name):
                i = work[name]
                assert i == n_work[0], (name, WORK[n_work[0]])
                n_work[0] += 1
                if i >= 4:
                    pe.wait_ge(*evac(WORK[i - 4][0]))
                return bank(name)

            def done(ins):
                ins.then_inc(product, 1)

            def weights(name):
                i = blk[name]
                pe.wait_ge(blk_in[i % WSLOTS], 16 * (i // WSLOTS + 1))
                return WR[:, i % WSLOTS, :, :]

            def tr(out, in_, k=P):
                return nc.tensor.transpose(out, in_, ident[0:k, 0:k])

            def vsums(c, par):
                if not (isinstance(c, int) and c < 2):
                    pe.wait_ge(updated, 2 * c - 2)
                for s in range(TOPK):
                    pe.wait_ge(v_in[s % NV], 16 * (2 * c + s // NV + 1))
                    pe.wait_ge(diag, c * TOPK + s + 1)
                    for hf in range(2):
                        ins = nc.tensor.matmul(acc[:, par, hf * 512:hf * 512 + 512], DG[:, s % 4, :],
                                               V[:, s % NV, hf * 512:hf * 512 + 512],
                                               start=(s == 0), stop=(s == TOPK - 1))
                    ins.then_inc(vsum, 1)

            for s in SCHEDULE:
                kind = s[0]
                if kind == "prep":
                    pe.wait_ge(consts, 6)
                    pe.wait_ge(loaded["rows"], 96)
                    o = begin(("rows",))
                    tr(o[:, 0:96], R1[:, :], 96)
                    done(tr(o[:, 96:144], R2[:, :], 48))
                    pe.wait_ge(loaded["keys"], 64)
                    o = begin(("keys",))
                    for k in range(4):
                        ins = tr(o[:, k * P:k * P + P], KR[:, k, :])
                    done(ins)
                elif kind == "ada":
                    _, l, k = s
                    if k < HALVES:
                        if k == 0:
                            pe.wait_ge(silu_done, 1)
                        o = begin(s)
                        for b in range(2):
                            w = weights(("ada", l, 2 * k + b))
                            for j in range(KC):
                                ins = nc.tensor.matmul(o[0:2, b * CW:(b + 1) * CW], SIL[:, :, j], w[:, j, :],
                                                       start=(j == 0), stop=(j == KC - 1))
                            if b == 0:
                                ins.then_inc(ada_first, 1)
                        done(ins)
                    if k > 0:
                        name = ("adaT", l, k - 1)
                        pe.wait_ge(*evac(("ada", l, k - 1)))
                        o = begin(name)
                        for i in range(4):
                            ins = tr(o[:, 2 * i:2 * i + 2], MROW[:, (k - 1) % 2, i * P:i * P + P], 2)
                        done(ins)
                elif kind == "hT":
                    _, l, which, st = s
                    pe.wait_ge(normed.sem, normed.at("norm", l, which, st))
                    for jj in range(KC // 2):
                        o = begin(s + (jj,))
                        for c in range(2):
                            for tt in range(2):
                                ins = tr(o[:, c * 256 + tt * P:c * 256 + tt * P + P],
                                         H[:, 2 * st + tt, (2 * jj + c) * P:(2 * jj + c + 1) * P])
                        done(ins)
                elif kind == "in":
                    _, l, b = s
                    w = weights(s)
                    for st in in_streams(l, b):
                        pe.wait_ge(*evac(("hT", l, 1, st, KC // 2 - 1)))
                        o = begin(s + (st,))
                        for tt in range(2):
                            for j in range(KC):
                                ins = nc.tensor.matmul(o[:, tt * CW:(tt + 1) * CW],
                                                       HT[:, j, (2 * st + tt) * P:(2 * st + tt + 1) * P], w[:, j, :],
                                                       start=(j == 0), stop=(j == KC - 1))
                        done(ins)
                elif kind == "tqk":
                    _, l, st = s
                    for tt in range(2):
                        if (l, st) != (1, CTX):
                            pe.wait_ge(roped.sem, roped.at("rope", l, 2 * st + tt))
                    pe.wait_ge(*evac(("in", l, 5, st)))
                    for name, _ in WORK:
                        if name[:3] == s:
                            o = begin(name)
                            for c in range(2):
                                for tt in range(2):
                                    i = 2 * name[4] + c
                                    cols = slice(c * 256 + tt * P, c * 256 + tt * P + P)
                                    if name[3] == "q":
                                        ins = tr(o[:, cols], QKV[:, 2 * st + tt, QOFF[l] + i * P:QOFF[l] + (i + 1) * P])
                                    else:
                                        src = QKV[:, 2 * st + tt, KOFF + i * HD:KOFF + (i + 1) * HD]
                                        for q0 in (0, 64):
                                            ins = nc.tensor.matmul(o[q0:q0 + 64, cols], src, ident[:, :],
                                                                   start=True, stop=True)
                            done(ins)
                elif kind == "att":
                    _, l, st = s
                    us = units(l, st)
                    group = QH[l] // NKV
                    k0, nk = (0, 512) if st == LAT else (256, 256)
                    for stq in (LAT, CTX):
                        pe.wait_ge(*evac(("tqk", l, stq, "k", 1)))
                    for a, i in att_steps(len(us)):
                        tt, h = us[i]
                        name = s + (a, i)
                        if a == "A":
                            o = begin(name)
                            q0 = 64 * (h % 2)
                            masked = l == 1
                            ins = nc.tensor.matmul(o[:, 0:nk], qT[q0:q0 + 64, h // 2, st * 256 + tt * P:st * 256 + tt * P + P],
                                                   kT[q0:q0 + 64, h // group, k0:k0 + nk], start=True, stop=not masked)
                            if masked:
                                m0 = P * (1 - tt)
                                ins = nc.tensor.matmul(o[:, m0:m0 + P], ident[:, :], MK[:, tt, :], start=False, stop=True)
                        elif a == "B":
                            pe.wait_ge(scaled.sem, scaled.at(l, st, i))
                            o = begin(name)
                            for kc in range(nk // P):
                                ins = tr(o[:, kc * P:kc * P + P], PR[:, i % 2, kc * P:kc * P + P])
                        else:
                            pe.wait_ge(*evac(s + ("B", i)))
                            o = begin(name)
                            q0 = 64 * (h % 2)
                            kv = h // group
                            for kc in range(nk // P):
                                vt = kc if st == LAT else kc + 2
                                ins = nc.tensor.matmul(o[q0:q0 + 64, 0:P], QKV[:, vt, VOFF + kv * HD:VOFF + (kv + 1) * HD],
                                                       PT[:, i % 2, kc * P:kc * P + P], start=(kc == 0), stop=(kc == nk // P - 1))
                        done(ins)
                elif kind == "pool":
                    st = s[1]
                    pe.wait_ge(loaded["pm"], 16)
                    pe.wait_ge(loaded["small"], 96)
                    for a, g in pool_steps():
                        name = s + (a, g)
                        if a == "PA":
                            o = begin(name)
                            for tt in range(2):
                                ins = nc.tensor.matmul(o[0:64, 0:256], QKV[:, 2 * st + tt, g * 64:g * 64 + 64], PM[:, tt, g, :],
                                                       start=(tt == 0), stop=(tt == 1))
                        else:
                            pe.wait_ge(*evac(s + ("PA", g)))
                            o = begin(name)
                            q0 = 64 * (g % 2)
                            ins = nc.tensor.matmul(o[q0:q0 + 64, 0:256], PW[:, g, :], PL[0:64, g % 2, :], start=True, stop=True)
                        done(ins)
                elif kind == "bc":
                    _, l, st = s
                    pe.wait_ge(*evac(("adaT", l, HALVES - 1)))
                    for v in (G1, SC2, SH2, G2):
                        for hf in range(2):
                            o = begin(s + (v, hf))
                            for i in range(4):
                                j = 4 * hf + i
                                ins = nc.tensor.matmul(o[:, i * P:i * P + P],
                                                       MOD[:, l, v * 8 + j, st:st + 1].to_broadcast([P, P]), ident[:, :],
                                                       start=True, stop=True)
                            done(ins)
                elif kind == "out":
                    _, l, st = s
                    pe.wait_ge(*evac(("att", l, st, "C", len(units(l, st)) - 1)))
                    if l == 0:
                        pe.wait_ge(*evac(("pool", st, "PB", 3)))
                    for b in range(D // CW):
                        w = weights(s + (b,))
                        o = begin(s + (b,))
                        for tt in range(2):
                            for j in range(KC):
                                ins = nc.tensor.matmul(o[:, tt * CW:(tt + 1) * CW], YT[st][:, j, tt * P:tt * P + P], w[:, j, :],
                                                       start=(j == 0), stop=(j == KC - 1))
                        done(ins)
                elif kind == "score":
                    _, l, st, heads = s
                    pe.wait_ge(*evac(("hT", l, 2, st, KC // 2 - 1)))
                    for a, h in score_steps(heads):
                        name = ("score", l, st, a, h)
                        if a == "Q":
                            w = weights(("wq", l, st, h))
                            o = begin(name)
                            for half in range(2):
                                for j in range(KC):
                                    ins = nc.tensor.matmul(o[:, half * 256:half * 256 + 256], w[:, j, half * P:half * P + P],
                                                           HT[:, j, st * 256:st * 256 + 256], start=(j == 0), stop=(j == KC - 1))
                            done(ins)
                        else:
                            pe.wait_ge(*evac(("score", l, st, "Q", h)))
                            o = begin(name)
                            for tt in range(2):
                                for half in range(2):
                                    ins = nc.tensor.matmul(o[:, (2 * tt + half) * P:(2 * tt + half + 1) * P],
                                                           QS[:, h % 2, half, tt * P:tt * P + P], KT[:, 2 * l + half, :],
                                                           start=True, stop=True)
                            done(ins)
                elif kind == "experts":
                    _, l, tile, part = s
                    c0 = chunk0(l, tile)
                    if part == 0:
                        if tile > 0:
                            vsums(c0 - 1, 1)
                        vsums(c0, 0)
                    else:
                        with pe.Fori(1, PH // 2) as p:
                            vsums(c0 + 2 * p - 1, 1)
                            vsums(c0 + 2 * p, 0)
                elif kind == "experts_end":
                    vsums(chunk0(s[1], TILES[s[1]][-1]) + PH - 1, 1)


INPUTS = ["x", "c", "ctx", "c_ctx", "ada_w", "ada_b", "norm1_g", "norm2_g", "final_g", "e_w_in", "e_q_norm_g",
          "e_k_norm_g", "e_pool_w", "e_pool_scale", "e_w_out", "o_w_in", "o_sink", "o_w_out", "p_w_q", "p_keys1",
          "p_keys2", "p_u", "p_v"]


def shape_constants(seq, head_dim):
    import numpy as np
    grid_w, half = 64, head_dim // 2
    pos = np.arange(seq)
    inv = (1.0 / (np.float32(10000.0) ** (np.arange(0, half, 2, dtype=np.float32) / np.float32(half)))).astype(np.float32)
    rope = np.zeros((2, 128, 2, head_dim), np.float32)
    for axis, coord in enumerate((pos // grid_w, pos % grid_w)):
        ang = coord.astype(np.float32)[:, None] * inv[None, :]
        cos, sin = np.cos(ang).astype(np.float32), np.sin(ang).astype(np.float32)
        o = axis * half
        c = np.concatenate([cos, cos], 1).reshape(2, 128, half)
        s = np.concatenate([-sin, sin], 1).reshape(2, 128, half)
        rope[:, :, 0, o:o + half] = c
        rope[:, :, 1, o:o + half] = s
    pm = np.zeros((4, seq, seq), np.float32)
    for g, w in enumerate((2, 4, 8, 16)):
        for q in range(seq):
            lo, hi = max(q - w // 2, 0), min(q + w - w // 2, seq)
            pm[g, lo:hi, q] = np.float32(1.0) / np.float32(hi - lo)
            pm[g, q, q] -= 1.0
    pool = pm.reshape(4, 2, 128, seq).transpose(2, 1, 0, 3)
    return np.ascontiguousarray(rope.transpose(1, 0, 2, 3)), np.ascontiguousarray(pool)


def kernel(**inputs):
    import numpy as np
    import concourse.bacc as bacc
    from concourse.bass_utils import run_bass_kernel_spmd as run

    nc = bacc.Bacc("TRN2", target_bir_lowering=False, num_devices=1)
    arrays, tensors = {}, {}
    rope, pool_m = shape_constants(256, 64)
    for name in INPUTS + ["rope", "pool_m"]:
        a = {"rope": rope, "pool_m": pool_m}[name] if name in ("rope", "pool_m") else np.ascontiguousarray(inputs[name])
        arrays[f"in_{name}"] = a
        tensors[name] = nc.dram_tensor(f"in_{name}", a.shape, mybir.dt.from_np(a.dtype), kind="ExternalInput").ap()
    tensors["out"] = nc.dram_tensor("out_x", (1, 256, 1024), F32, kind="ExternalOutput").ap()
    program(nc, tensors)
    r = run(nc, [arrays], core_ids=[0])
    return r.results[0]["out_x"]
```

```python
from contextlib import ExitStack

import concourse.bass as bass
from concourse import mybir

F32 = mybir.dt.float32
U32 = mybir.dt.uint32
I32 = mybir.dt.int32
ALU = mybir.AluOpType
ACT = mybir.ActivationFunctionType
AX = mybir.AxisListType

P = 128
D = 1024
KC = D // P
DEPTH = 2
LAT, CTX = 0, 1
HD = 64
NKV = 4
QH = (12, 16)
QOFF = (256, 0)
KOFF, VOFF, DIN = 1024, 1280, 1536
CW = 256
WSLOTS = 3
EPS = 1e-6
PH = 8
TOPK = 16
NKEYS = 128
NEXP = NKEYS * NKEYS
NU = NV = 8
PAIR = 2 * TOPK
CAND = [(0, 1, 16), (1, 1, 8), (2, 1, 5), (3, 1, 4), (4, 1, 3), (5, 3, 2), (8, 8, 1)]
NCAND = sum(r * c for _, r, c in CAND)
SCALE = HD ** -0.5
LOWEST = -3.0e38
MASKED = -1e30 / SCALE
SH1, SC1, G1, SH2, SC2, G2 = range(6)
HALVES = 12
TILES = ((0, 1, 2, 3), (0, 1))


def gather_stages(l, between):
    s = []
    for t in TILES[l]:
        for part in ("0", "1", "loop", "6", "7"):
            s += [("experts", l, t, part)] + between.get((t, part), [])
    return s + [("experts_end", l)]


def schedule():
    both = (LAT, CTX)
    s = [("prep",)] + [("ada", 0, k) for k in range(5)]
    s += [("norm", 0, 1, LAT), ("norm", 0, 1, CTX), ("hT", 0, 1, LAT), ("hT", 0, 1, CTX)]
    s += [("in", 0, 4, both), ("in", 0, 5, both), ("in", 0, 1, (LAT,)), ("in", 0, 2, (LAT,)), ("in", 0, 3, (LAT,)),
          ("in", 0, 0, both)]
    s += [("rope", 0, 0, "qk"), ("rope", 0, 1, "qk"), ("rope", 0, 2, "k"), ("rope", 0, 3, "k")]
    s += [("ada", 0, k) for k in range(5, HALVES + 1)]
    s += [("tqk", 0, LAT, "q"), ("tqk", 0, LAT, "k"), ("tqk", 0, CTX, "k")]
    s += [("pool", LAT), ("pool", CTX), ("att", 0, LAT, 0, 24)]
    s += [("bc", 0, LAT), ("out", 0, LAT), ("norm", 0, 2, LAT), ("hT", 0, 2, LAT)]
    s += [("score", 0, LAT, (0, 1, 2, 3)), ("topk", 0, 0, 0), ("score", 0, LAT, (4, 5, 6, 7))]
    s += gather_stages(0, {
        (0, "0"): [("topk", 0, 0, 1)],
        (0, "1"): [("in", 0, 1, (CTX,)), ("in", 0, 2, (CTX,)), ("in", 0, 3, (CTX,)),
                   ("rope", 0, 2, "q"), ("rope", 0, 3, "q")],
        (0, "loop"): [("tqk", 0, CTX, "q"), ("att", 0, CTX, 0, 12)],
        (0, "6"): [("topk", 0, 1, 0)],
        (0, "7"): [("att", 0, CTX, 12, 24)],
        (1, "0"): [("topk", 0, 1, 1), ("bc", 0, CTX)],
        (1, "1"): [("out", 0, CTX), ("norm", 0, 2, CTX), ("hT", 0, 2, CTX)],
        (1, "loop"): [("score", 0, CTX, (0, 1, 2, 3))],
        (1, "6"): [("topk", 0, 2, 0)],
        (1, "7"): [("score", 0, CTX, (4, 5, 6, 7))],
        (2, "0"): [("topk", 0, 2, 1)] + [("ada", 1, k) for k in range(3)],
        (2, "1"): [("norm", 1, 1, LAT)] + [("ada", 1, k) for k in range(3, 6)] + [("hT", 1, 1, LAT)],
        (2, "loop"): [("in", 1, 0, (LAT,)), ("in", 1, 1, (LAT,)), ("in", 1, 2, (LAT,))],
        (2, "6"): [("topk", 0, 3, 0)] + [("ada", 1, k) for k in range(6, 9)],
        (2, "7"): [("in", 1, 3, (LAT,)), ("in", 1, 4, (LAT,)), ("in", 1, 5, (LAT,))],
        (3, "0"): [("topk", 0, 3, 1)] + [("ada", 1, k) for k in range(9, 12)],
        (3, "1"): [("ada", 1, 12), ("rope", 1, 0, "qk"), ("rope", 1, 1, "qk"), ("tqk", 1, LAT, "q"), ("tqk", 1, LAT, "k")],
    })
    s += [("norm", 1, 1, CTX), ("hT", 1, 1, CTX), ("in", 1, 4, (CTX,)), ("in", 1, 5, (CTX,)), ("tqk", 1, CTX, "k")]
    s += [("att", 1, LAT, 0, 32), ("bc", 1, LAT), ("out", 1, LAT), ("norm", 1, 2, LAT), ("hT", 1, 2, LAT)]
    s += [("score", 1, LAT, (0, 1, 2, 3)), ("topk", 1, 0, 0), ("score", 1, LAT, (4, 5, 6, 7))]
    s += gather_stages(1, {(0, "0"): [("topk", 1, 0, 1)], (0, "loop"): [("topk", 1, 1, 0)], (0, "6"): [("topk", 1, 1, 1)]})
    return s + [("final",)]


SCHEDULE = schedule()


def units(l, st):
    return [(tt, h) for tt in range(2) for h in range(QH[l])]


def score_steps(heads):
    steps = [("Q", heads[0])]
    for i, h in enumerate(heads):
        if i + 1 < len(heads):
            steps.append(("Q", heads[i + 1]))
        steps.append(("R", h))
    return steps


def att_steps(lo, n):
    steps = [("A", lo), ("A", lo + 1)]
    for i in range(lo, n):
        steps.append(("B", i))
        if i + 2 < n:
            steps.append(("A", i + 2))
        steps.append(("C", i))
    return steps


def pool_steps():
    return [("PA", 0), ("PA", 1), ("PB", 0), ("PA", 2), ("PB", 1), ("PA", 3), ("PB", 2), ("PB", 3)]


def work_order():
    w = []
    for s in SCHEDULE:
        k = s[0]
        if k == "prep":
            w += [(("rows",), "act"), (("keys",), "act")]
        elif k == "ada":
            if s[2] < HALVES:
                w += [(("ada", s[1], s[2]), "act")]
            if s[2] > 0:
                w += [(("adaT", s[1], s[2] - 1), "dve")]
        elif k == "hT":
            w += [(s + (jj,), "act") for jj in range(KC // 2)]
        elif k == "in":
            w += [(s[:3] + (st,), "act") for st in s[3]]
        elif k == "tqk":
            w += [(s + (i,), "act") for i in range(QH[s[1]] // 4 if s[3] == "q" else NKV // 2)]
        elif k == "att":
            w += [(s[:3] + (a, i), {"A": "exp", "B": "act", "C": "dve"}[a]) for a, i in att_steps(s[3], s[4])]
        elif k == "pool":
            w += [(s + (a, g), "dve") for a, g in pool_steps()]
        elif k == "bc":
            w += [(s + (v, hf), "act") for v in (G1, SC2, SH2, G2) for hf in range(2)]
        elif k == "out":
            w += [(s + (b,), "dve") for b in range(D // CW)]
        elif k == "score":
            w += [(s[:3] + (a, h), "act") for a, h in score_steps(s[3])]
    return w


WORK = work_order()


def block_order():
    o = []
    for s in SCHEDULE:
        if s[0] == "ada" and s[2] < HALVES:
            o += [("ada", s[1], 2 * s[2] + i) for i in range(2)]
        elif s[0] == "in":
            o += [s]
        elif s[0] == "out":
            o += [s + (b,) for b in range(D // CW)]
        elif s[0] == "score":
            o += [("wq", s[1], s[2], h) for h in s[3]]
    return o


BLOCKS = block_order()


class Count:

    def __init__(self, sem, names):
        self.sem, self.pos = sem, {n: i + 1 for i, n in enumerate(names)}

    def at(self, *name):
        return self.pos[name]


def named(*kinds):
    return [s for s in SCHEDULE if s[0] in kinds]


def program(nc, t):
    x_d, c_d, ctx_d, cctx_d = t["x"], t["c"], t["ctx"], t["c_ctx"]
    out_d = t["out"]
    es = ExitStack()
    with es:
        def sb(name, shape, dt=F32):
            return es.enter_context(nc.sbuf_tensor(name, shape, dt))

        def sem(name):
            return es.enter_context(nc.semaphore(name))

        X = sb("X", [P, 4, D])
        H = sb("H", [P, 4, D])
        HT = sb("HT", [P, KC, 4 * P])
        BC = sb("BC", [P, 5, D])
        G1B, A2B, B2B, G2B = BC[:, 0, :], BC[:, 1, :], BC[:, 2, :], (BC[:, 3, :], BC[:, 4, :])
        WR = sb("WR", [P, WSLOTS, KC, CW])
        RING = sb("RING", [P, NU + NV, D])
        U, V = RING[:, 0:NU, :], RING[:, NU:NU + NV, :]
        QKVL = BC[:, 0:3, :].rearrange("p a b -> p (a b)").rearrange("p (t n) -> p t n", t=2)
        UN = RING[:, 2, 0:512].rearrange("p (t n) -> p t n", t=2)
        KN = RING[:, 2, 512:1024].rearrange("p (t n) -> p t n", t=2)
        VC = sb("VC", [P, 2, CW])
        QT = (H[:, 0:2, :].rearrange("p a b -> p (a b)").rearrange("p (c n) -> p c n", c=8), HT[:, :, 0:256])
        KTS = [G2B[st].rearrange("p (c n) -> p c n", c=NKV) for st in (LAT, CTX)]
        YT = [r_.rearrange("p a b -> p (a b)").rearrange("p (c n) -> p c n", c=8) for r_ in (RING[:, 0:2, :], H[:, 2:4, :])]
        SCR = sb("SCR", [P, 4096])
        SC = SCR[:, :].rearrange("p (t s n) -> p t s n", t=2, s=16)
        QNC = SCR[:, 0:1536].rearrange("p (t n) -> p t n", t=2)
        PR = (SCR[:, 0:1024].rearrange("p (r n) -> p r n", r=2), A2B[:, 0:512].rearrange("p (r n) -> p r n", r=2))
        PT = (SCR[:, 1024:2048].rearrange("p (r n) -> p r n", r=2), A2B[:, 512:1024].rearrange("p (r n) -> p r n", r=2))
        PM = SCR[:, 2048:4096].rearrange("p (i g n) -> p i g n", i=2, g=4)
        OHR = sb("OHR", [P, 3200])
        OH = OHR[:, :].rearrange("p (h k n) -> p h k n", h=4, k=TOPK)
        T1, T2 = OHR[:, 0:1280], OHR[:, 1280:2560]
        PL = OHR[:, 2560:3072].rearrange("p (r n) -> p r n", r=2)
        R1 = H[0:96, 0, 512:640]
        R2 = H[0:48, 0, 640:768]
        CT = sb("CT", [P, 144])
        KR = H[:, 0, 0:512].rearrange("p (k n) -> p k n", k=4)
        KT = sb("KT", [P, 4, P])
        SIL = sb("SIL", [P, 2, KC])
        SE = sb("SE", [P, 2, KC])
        MOD = sb("MOD", [P, DEPTH, 48, 2])
        RC = sb("RC", [P, 2, 2, HD])
        GN = sb("GN", [P, 2, HD])
        CG = RING[:, 9, 0:512].rearrange("p (t q c n) -> p t q c n", t=2, q=2, c=2)
        PW = RING[0:HD, 9, 512:768].rearrange("p (g n) -> p g n", g=4)
        SK = sb("SK", [P, 16])
        PS = sb("PS", [P, 2])
        ident = sb("ident", [P, P])
        MK = sb("MK", [P, 2, P])
        EPT = sb("EPT", [P, 1])
        SS = sb("SS", [P, 2])
        RS = sb("RS", [P, 2])
        HS = sb("HS", [P, 16])
        HR = sb("HR", [P, 16])
        STM = sb("STM", [P, 4, 4])
        QS = sb("QS", [P, 2, 2, 2 * P])
        MROW = QS[0:2, :, :, :].rearrange("p r a n -> p r (a n)")
        TV = sb("TV", [P, 2, 4, TOPK])
        TI = sb("TI", [P, 2, 4, TOPK], U32)
        TF = sb("TF", [P, 2, 4, TOPK])
        CA = sb("CA", [P, 4, NCAND])
        CI = sb("CI", [P, 4, NCAND])
        SV = sb("SV", [P, 4, TOPK])
        PI = sb("PI", [P, 4, TOPK], U32)
        PF = sb("PF", [P, 4, TOPK])
        IF = sb("IF", [P, 4, TOPK])
        SM = sb("SM", [P, 4])
        IOI = sb("IOI", [P, NCAND], I32)
        IOF = sb("IOF", [P, NCAND])
        IDX = sb("IDX", [P, 2, PH * TOPK], U32)
        WG = sb("WG", [P, 2, PH * TOPK])
        IU = sb("IU", [P, 2, TOPK], U32)
        IV = sb("IV", [P, 2, TOPK], U32)
        A = sb("A", [P, 2, TOPK])
        GA = sb("GA", [P, 2, TOPK])
        WT = sb("WT", [P, 2, TOPK])
        DG = sb("DG", [P, 4, P])
        acc = es.enter_context(nc.psum_tensor("acc", [P, 2, D], F32))
        wk = es.enter_context(nc.psum_tensor("wk", [P, 4, 512], F32))

        loaded = {n: sem("ld_" + n) for n in ("rows", "keys", "x", "ctx", "small", "pm")}
        final_gain = sem("final_gain")
        blk_in = [sem(f"blk{i}") for i in range(WSLOTS)]
        ada_first = sem("ada_first")
        product = sem("product")
        act_evac, dve_evac = sem("act_evac"), sem("dve_evac")
        consts = sem("consts")
        exp_c, silu_done = sem("exp_c"), sem("silu_done")
        norms = [s for s in SCHEDULE if s[0] in ("norm", "final")]
        sumsq = Count(sem("sumsq"), norms)
        sqrted = Count(sem("sqrted"), norms)
        normed = Count(sem("normed"), norms)
        ropes = named("rope")
        hsumsq = Count(sem("hsumsq"), [s for s in ropes if s[1] == 0])
        hsqrt = Count(sem("hsqrt"), [s for s in ropes if s[1] == 0])
        roped = Count(sem("roped"), ropes)
        all_units = [(s[1], s[2], i) for s in named("att") for i in range(s[3], s[4])]
        maxed = Count(sem("maxed"), all_units)
        expd = Count(sem("expd"), all_units)
        scaled = Count(sem("scaled"), all_units)
        topks = named("topk")
        shifted = Count(sem("shifted"), topks)
        texp = Count(sem("texp"), topks)
        chosen = Count(sem("chosen"), topks)
        scores_used = Count(sem("scores_used"), topks)
        u_in = [sem(f"u_in{i}") for i in range(NU)]
        v_in = [sem(f"v_in{i}") for i in range(NV)]
        ixcopy, issued, gate_sem = sem("ixcopy"), sem("issued"), sem("gate_sem")
        dotted, gelud, weighted, diag, vsum, updated = (sem(n) for n in (
            "dotted", "gelud", "weighted", "diag", "vsum", "updated"))
        dch, ach = sem("dch"), sem("ach")
        stored = sem("stored")

        work = {n: i for i, (n, _) in enumerate(WORK)}

        def evac(name):
            i = work[name]
            e = WORK[i][1]
            if e == "exp":
                return expd.sem, expd.at(name[1], name[2], name[4])
            return (act_evac if e == "act" else dve_evac), sum(1 for _, x in WORK[:i + 1] if x == e)

        def bank(name):
            return wk[:, work[name] % 4, :]

        blk = {n: i for i, n in enumerate(BLOCKS)}

        def block_used(name):
            kind, l, b = name[0], name[1], name[2] if name[0] == "in" else name[-1]
            if kind == "ada" and b % 2 == 0:
                return ada_first, HALVES * l + b // 2 + 1
            last = ("ada", l, b // 2) if kind == "ada" else name[:3] + name[3][-1:] if kind == "in" else \
                ("score",) + name[1:3] + ("Q", b) if kind == "wq" else name
            return product, work[last] + 1

        def chunk0(l, t):
            return 32 * l + PH * t

        block = es.enter_context(nc.Block())

        @block.sync
        def _(sp):
            rows = [(R1[0:8], c_d.rearrange("o (j p) -> (o j) p", p=P)),
                    (R1[8:16], cctx_d.rearrange("(j p) -> j p", p=P)),
                    (R1[16:32], t["norm1_g"].rearrange("l (j p) -> (l j) p", p=P)),
                    (R1[32:48], t["norm2_g"].rearrange("l (j p) -> (l j) p", p=P)),
                    (R1[48:96], t["ada_b"][0].rearrange("(j p) -> j p", p=P)),
                    (R2[:, :], t["ada_b"][1].rearrange("(j p) -> j p", p=P))]
            for dst, src in rows:
                sp.dma_start(dst, src).then_inc(loaded["rows"], 16)
            for l in range(DEPTH):
                sp.dma_start(KR[:, 2 * l, :], t["p_keys1"][l]).then_inc(loaded["keys"], 16)
                sp.dma_start(KR[:, 2 * l + 1, :], t["p_keys2"][l]).then_inc(loaded["keys"], 16)
            srcs = {"ada": t["ada_w"], "out": (t["e_w_out"], t["o_w_out"]), "in": (t["e_w_in"], t["o_w_in"]),
                    "wq": t["p_w_q"]}
            for i, name in enumerate(BLOCKS):
                if i == 2:
                    sp.dma_start(X[:, 0:2, :], x_d[0].rearrange("(a p) d -> p a d", p=P)).then_inc(loaded["x"], 16)
                    sp.dma_start(X[:, 2:4, :], ctx_d[0].rearrange("(a p) d -> p a d", p=P)).then_inc(loaded["ctx"], 16)
                if i == 4:
                    sp.dma_start(RC[:, :, :, :], t["rope"]).then_inc(loaded["small"], 16)
                    sp.dma_start(GN[:, 0, :], t["e_q_norm_g"].partition_broadcast(P)[:, 0, :]).then_inc(loaded["small"], 16)
                    sp.dma_start(GN[:, 1, :], t["e_k_norm_g"].partition_broadcast(P)[:, 0, :]).then_inc(loaded["small"], 16)
                    sp.dma_start(SK[:, :], t["o_sink"].partition_broadcast(P)[:, 0, :]).then_inc(loaded["small"], 16)
                    sp.dma_start(PW[:, :, :], t["e_pool_w"][0].rearrange("g c d -> c g d")).then_inc(loaded["small"], 16)
                    with nc.allow_non_contiguous_dma(reason="256 words"):
                        sp.dma_start(PS[:, :], t["e_pool_scale"][0].rearrange("(j p) -> p j", p=P)).then_inc(loaded["small"], 16)
                    sp.dma_start(PM[:, :, :, :], t["pool_m"]).then_inc(loaded["pm"], 16)
                if i >= WSLOTS:
                    sp.wait_ge(*block_used(BLOCKS[i - WSLOTS]))
                kind, l, b = name[0], name[1], name[2] if name[0] == "in" else name[-1]
                w = srcs[kind][0] if (kind in ("in", "out") and l == 0) else \
                    srcs[kind][1] if kind in ("in", "out") else srcs[kind][l]
                if kind in ("in", "out"):
                    w = w[0]
                sp.dma_start(WR[:, i % WSLOTS, :, :],
                             w.rearrange("(j p) n -> p j n", p=P)[:, :, b * CW:(b + 1) * CW]).then_inc(blk_in[i % WSLOTS], 16)
            sp.wait_ge(normed.sem, normed.at("norm", 1, 2, LAT))
            sp.wait_ge(*evac(("out", 1, LAT, D // CW - 1)))
            sp.dma_start(G1B, t["final_g"].partition_broadcast(P)).then_inc(final_gain, 16)
            sp.wait_ge(normed.sem, normed.at("final"))
            sp.dma_start(out_d[0].rearrange("(a p) d -> p a d", p=P), H[:, 0:2, :]).then_inc(stored, 16)
            sp.wait_ge(stored, 16)

        @block.gpsimd
        def _(pool):
            nc.gpsimd.memset(ident[:, :], 0.0).then_inc(consts, 1)
            nc.gpsimd.memset(MK[:, :, :], 0.0).then_inc(consts, 1)
            pool.wait_ge(consts, 2)
            nc.gpsimd.affine_select(out=ident[:, :], in_=ident[:, :], compare_op=ALU.not_equal, fill=1.0,
                                    base=0, pattern=[[-1, P]], channel_multiplier=1).then_inc(consts, 1)
            nc.gpsimd.affine_select(out=MK[:, 0, :], in_=MK[:, 0, :], compare_op=ALU.is_ge, fill=MASKED,
                                    base=0, pattern=[[-1, P]], channel_multiplier=1).then_inc(consts, 1)
            nc.gpsimd.affine_select(out=MK[:, 1, :], in_=MK[:, 1, :], compare_op=ALU.is_ge, fill=MASKED,
                                    base=0, pattern=[[1, P]], channel_multiplier=-1).then_inc(consts, 1)
            nc.gpsimd.iota(IOI[:, :], pattern=[[1, NCAND]], base=0, channel_multiplier=0).then_inc(consts, 1)
            tables = {"u": t["p_u"].rearrange("l n d -> (l n) d"), "v": t["p_v"].rearrange("l n d -> (l n) d")}

            def gate(s, value):
                pool.wait_ge(s, value)
                pool.sem_inc(gate_sem, 1)

            def copy_rows(dst, tile, col):
                nc.gpsimd.tensor_copy(dst, IDX[:, tile % 2, col]).then_inc(ixcopy, 1)

            def gather(table, ring, n, rows, slot_in):
                pool.indirect_dma_start(out=ring[:, n % NU, :], out_offset=None, in_=tables[table],
                                        in_offset=bass.IndirectOffsetOnAxis(ap=rows, axis=0),
                                        engine_sem=issued).then_inc(slot_in[n % NU], 16)

            def chunk(l, tile, p, hh, vtile, vcol, first):
                c = chunk0(l, tile) + 2 * p + hh
                start = first and hh == 0 and tile == 0
                static = isinstance(p, int)
                if not (static and c < 2):
                    (gate)(issued, 32 * c - 48)
                col = (2 * p + hh) * TOPK
                copy_rows(IU[:, hh, :], tile, slice(col, col + TOPK) if static else bass.ds(col, TOPK))
                if not start:
                    copy_rows(IV[:, 1 - hh, :], vtile, vcol)
                gate(ixcopy, 2 * c + 1)
                for s in range(TOPK):
                    if not (static and c == 0 and s < NU):
                        gate(dotted, c * TOPK + s - NU + 1)
                    gather("u", U, s, IU[:, hh, s:s + 1], u_in)
                    if not start:
                        if not (static and c == 1 and s < NV):
                            gate(vsum, (c - 1) * TOPK + s - NV + 1)
                        gather("v", V, s, IV[:, 1 - hh, s:s + 1], v_in)

            for s in SCHEDULE:
                if s[0] == "experts":
                    _, l, tile, part = s
                    if part == "0":
                        pool.wait_ge(chosen.sem, chosen.at("topk", l, tile, 0))
                        chunk(l, tile, 0, 0, tile - 1, slice(7 * TOPK, 8 * TOPK), True)
                    elif part == "loop":
                        pool.wait_ge(chosen.sem, chosen.at("topk", l, tile, 1))
                        with pool.Fori(1, PH // 2 - 1) as p:
                            chunk(l, tile, p, 0, tile, bass.ds((2 * p - 1) * TOPK, TOPK), False)
                            chunk(l, tile, p, 1, tile, bass.ds(2 * p * TOPK, TOPK), False)
                    else:
                        h = int(part)
                        chunk(l, tile, h // 2, h % 2, tile, slice((h - 1) * TOPK, h * TOPK), False)
                elif s[0] == "experts_end":
                    l = s[1]
                    tile = TILES[l][-1]
                    c = chunk0(l, tile) + PH
                    pool.wait_ge(issued, 32 * c - 48)
                    copy_rows(IV[:, 1, :], tile, slice(7 * TOPK, 8 * TOPK))
                    pool.wait_ge(ixcopy, 2 * c)
                    for s_ in range(TOPK):
                        pool.wait_ge(vsum, (c - 1) * TOPK + s_ - NV + 1)
                        gather("v", V, s_, IV[:, 1, s_:s_ + 1], v_in)

        @block.vector
        def _(dve):
            last = [None, 0]

            def op(ins, s=None, value=None):
                if s is None:
                    last[1] += 1
                    ins.then_inc(dch, 1)
                    last[0] = (dch, last[1])
                else:
                    ins.then_inc(s, 1)
                    last[0] = (s, value)

            def after():
                dve.wait_ge(*last[0])

            def taken(ins, name):
                op(ins, *evac(name))

            def ready(name):
                dve.wait_ge(product, work[name] + 1)

            def topk16(vals, idxs, rows):
                op(nc.vector.max(out=vals[:, 0:8], in_=rows))
                after()
                op(nc.vector.max_index(out=idxs[:, 0:8], in_max=vals[:, 0:8], in_values=rows))
                after()
                op(nc.vector.match_replace(out=rows, in_to_replace=vals[:, 0:8], in_values=rows, imm_value=LOWEST))
                after()
                op(nc.vector.max(out=vals[:, 8:16], in_=rows))
                after()
                op(nc.vector.max_index(out=idxs[:, 8:16], in_max=vals[:, 8:16], in_values=rows))

            def dots(c, hh, tile):
                for s in range(TOPK):
                    dve.wait_ge(u_in[s % NU], 16 * (2 * c + s // NU + 1))
                    nc.vector.scalar_tensor_tensor(out=U[:, s % NU, :], in0=U[:, s % NU, :], scalar=1.0,
                                                   in1=H[:, tile, :], op0=ALU.mult, op1=ALU.mult,
                                                   accum_out=A[:, hh, s:s + 1]).then_inc(dotted, 1)

            def update(c, par, tile):
                g2 = G2B[tile // 2]
                dve.wait_ge(vsum, (c + 1) * TOPK)
                nc.vector.tensor_tensor(acc[:, par, :], acc[:, par, :], g2, ALU.mult).then_inc(updated, 1)
                dve.wait_ge(updated, 2 * c + 1)
                nc.vector.tensor_tensor(X[:, tile, :], X[:, tile, :], acc[:, par, :], ALU.add).then_inc(updated, 1)

            def chunk(l, tile, p, hh, vtile, start):
                c = chunk0(l, tile) + 2 * p + hh
                dots(c, hh, tile)
                dve.wait_ge(gelud, c + 1)
                col = (2 * p + hh) * TOPK
                g = WG[:, tile % 2, col:col + TOPK] if isinstance(p, int) else WG[:, tile % 2, bass.ds(col, TOPK)]
                nc.vector.tensor_tensor(WT[:, hh, :], GA[:, hh, :], g, ALU.mult).then_inc(weighted, 1)
                if not start:
                    update(c - 1, 1 - hh, vtile)

            for s in SCHEDULE:
                kind = s[0]
                if kind == "prep":
                    op(nc.vector.memset(EPT[:, :], EPS))
                    dve.wait_ge(consts, 6)
                    op(nc.vector.tensor_copy(IOF[:, :], IOI[:, :]))
                    dve.wait_ge(exp_c, 1)
                    op(nc.vector.tensor_scalar_add(SE[:, :, :], SE[:, :, :], 1.0))
                    after()
                    op(nc.vector.reciprocal(SE[:, :, :], SE[:, :, :]))
                    after()
                    op(nc.vector.tensor_tensor(SIL[:, :, :], SE[:, :, :],
                                               CT[:, 0:16].rearrange("p (s j) -> p s j", s=2), ALU.mult), silu_done, 1)
                    dve.wait_ge(loaded["small"], 96)
                    for tt in range(2):
                        cosb = RC[:, tt, 0, :].unsqueeze(1).to_broadcast([P, 2, HD])
                        op(nc.vector.tensor_tensor(CG[:, tt, :, 0, :], GN[:, :, :], cosb, ALU.mult))
                        for a in range(2):
                            for q in range(2):
                                o = CG[:, tt, q, 1, :].rearrange("p (h a n) -> p h a n", h=2, a=2)[:, :, a, :]
                                sn = RC[:, tt, 1, :].rearrange("p (h a n) -> p h a n", h=2, a=2)[:, :, a, :]
                                g = GN[:, q, :].rearrange("p (h a n) -> p h a n", h=2, a=2)[:, :, 1 - a, :]
                                op(nc.vector.tensor_tensor(o, sn, g, ALU.mult))
                elif kind == "ada" and s[2] > 0:
                    l, k = s[1], s[2] - 1
                    name = ("adaT", l, k)
                    ready(name)
                    cols = MOD[:, l, 4 * k:4 * k + 4, :]
                    bias = CT[:, 48 + 48 * l + 4 * k:48 + 48 * l + 4 * k + 4].unsqueeze(2).to_broadcast([P, 4, 2])
                    add = nc.vector.tensor_tensor(cols, bank(name)[:, 0:8].rearrange("p (k s) -> p k s", s=2), bias, ALU.add)
                    if k // 2 in (SC1, SC2):
                        op(add)
                        after()
                        g0 = (16 if k // 2 == SC1 else 32) + 8 * l + 4 * (k % 2)
                        gain = CT[:, g0:g0 + 4].unsqueeze(2).to_broadcast([P, 4, 2])
                        taken(nc.vector.scalar_tensor_tensor(out=cols, in0=cols, scalar=1.0, in1=gain,
                                                             op0=ALU.add, op1=ALU.mult), name)
                    else:
                        taken(add, name)
                elif kind in ("norm", "final"):
                    st = s[3] if kind == "norm" else LAT
                    if s == ("norm", 0, 1, LAT):
                        dve.wait_ge(loaded["x"], 16)
                        dve.wait_ge(*evac(("keys",)))
                    if s == ("norm", 0, 1, CTX):
                        dve.wait_ge(loaded["ctx"], 16)
                    if last[0] is not None:
                        after()
                    for tt in range(2):
                        ins = nc.vector.scalar_tensor_tensor(
                            out=H[:, 2 * st + tt, :], in0=X[:, 2 * st + tt, :], scalar=1.0, in1=X[:, 2 * st + tt, :],
                            op0=ALU.mult, op1=ALU.mult, accum_out=SS[:, tt:tt + 1])
                        if tt == 0:
                            op(ins)
                    op(ins, sumsq.sem, sumsq.at(*s))
                    dve.wait_ge(sqrted.sem, sqrted.at(*s))
                    op(nc.vector.reciprocal(RS[:, :], SS[:, :]))
                    after()
                    if kind == "norm" and s[2] == 2:
                        dve.wait_ge(*evac(("bc", s[1], st, SH2, 1)))
                    if kind == "final":
                        dve.wait_ge(final_gain, 16)
                    for tt in range(2):
                        h, x, r = H[:, 2 * st + tt, :], X[:, 2 * st + tt, :], RS[:, tt:tt + 1]
                        if kind == "norm" and s[2] == 1:
                            ins = nc.vector.tensor_scalar(h, x, r, None, ALU.mult)
                        elif kind == "final":
                            ins = nc.vector.scalar_tensor_tensor(out=h, in0=x, scalar=r, in1=G1B, op0=ALU.mult, op1=ALU.mult)
                        else:
                            op(nc.vector.scalar_tensor_tensor(out=h, in0=x, scalar=r, in1=A2B, op0=ALU.mult, op1=ALU.mult))
                            after()
                            ins = nc.vector.tensor_tensor(h, h, B2B, ALU.add)
                        if tt == 0:
                            op(ins)
                    op(ins, normed.sem, normed.at(*s))
                elif kind == "rope":
                    l, tile = s[1], s[2]
                    st, tt = tile // 2, tile % 2
                    for b in (1, 2, 3, 4):
                        if st == LAT or (b == 4) == (s[3] == "k"):
                            dve.wait_ge(*evac(("in", l, b, st)))
                    after()
                    nh = {"qk": 16 if l == 0 else 20, "q": 12, "k": 4}[s[3]]
                    R = QKVL[:, tt, QOFF[l]:QOFF[l] + nh * HD] if st == LAT else QNC[:, tt, :] if s[3] == "q" else KN[:, tt, :]
                    R = R.rearrange("p (h n) -> p h n", n=HD)
                    a1 = T1[:, 0:nh * HD].rearrange("p (h n) -> p h n", n=HD)
                    a2 = T2[:, 0:nh * HD].rearrange("p (h n) -> p h n", n=HD)
                    if l == 0:
                        op(nc.vector.tensor_tensor(a1, R, R, ALU.mult))
                        after()
                        op(nc.vector.tensor_reduce(out=HS[:, 0:nh], in_=a1, axis=AX.X, op=ALU.add), hsumsq.sem, hsumsq.at(*s))
                        dve.wait_ge(hsqrt.sem, hsqrt.at(*s))
                        op(nc.vector.reciprocal(HR[:, 0:nh], HS[:, 0:nh]))
                        after()
                        op(nc.vector.tensor_tensor(R, R, HR[:, 0:nh].unsqueeze(2).to_broadcast([P, nh, HD]), ALU.mult))
                        after()
                        groups = {"qk": [(0, 12, 0), (12, 16, 1)], "q": [(0, 12, 0)], "k": [(0, 4, 1)]}[s[3]]
                    else:
                        groups = [(0, 20, None)]
                    if st == CTX:
                        (lo, hi, q), = groups
                        op(nc.vector.tensor_tensor(R, R, GN[:, q, :].unsqueeze(1).to_broadcast([P, nh, HD]), ALU.mult),
                           roped.sem, roped.at(*s))
                    else:
                        for lo, hi, q in groups:
                            tab = RC[:, tt, :, :] if q is None else CG[:, tt, q, :, :]
                            op(nc.vector.tensor_tensor(a1[:, lo:hi, :], R[:, lo:hi, :],
                                                       tab[:, 0, :].unsqueeze(1).to_broadcast([P, hi - lo, HD]), ALU.mult))
                            for a in range(2):
                                for half in range(2):
                                    o = 32 * half + 16 * a
                                    i = 32 * half + 16 * (1 - a)
                                    op(nc.vector.tensor_tensor(
                                        a2[:, lo:hi, o:o + 16], R[:, lo:hi, i:i + 16],
                                        tab[:, 1, o:o + 16].unsqueeze(1).to_broadcast([P, hi - lo, 16]), ALU.mult))
                        after()
                        op(nc.vector.tensor_tensor(R, a1, a2, ALU.add), roped.sem, roped.at(*s))
                elif kind == "att":
                    _, l, st, i0, n = s
                    us = units(l, st)
                    nk = 512 if st == LAT else 256

                    def rowmax(i):
                        name = s[:3] + ("A", i)
                        tt, h = us[i]
                        ready(name)
                        op(nc.vector.reduce_max(STM[:, i % 4, 0:1], bank(name)[:, 0:nk], AX.X))
                        after()
                        if l == 0:
                            op(nc.vector.tensor_scalar(STM[:, i % 4, 1:2], STM[:, i % 4, 0:1], -SCALE, None, ALU.mult),
                               maxed.sem, maxed.at(l, st, i))
                        else:
                            op(nc.vector.tensor_scalar(STM[:, i % 4, 1:2], STM[:, i % 4, 0:1], SCALE, SK[:, h:h + 1],
                                                       ALU.mult, ALU.max))
                            after()
                            op(nc.vector.tensor_scalar(STM[:, i % 4, 1:2], STM[:, i % 4, 1:2], -1.0, None, ALU.mult),
                               maxed.sem, maxed.at(l, st, i))

                    def rescale(i):
                        dve.wait_ge(expd.sem, expd.at(l, st, i))
                        if l == 1:
                            op(nc.vector.tensor_tensor(STM[:, i % 4, 2:3], STM[:, i % 4, 2:3], STM[:, i % 4, 3:4], ALU.add))
                            after()
                        op(nc.vector.reciprocal(STM[:, i % 4, 2:3], STM[:, i % 4, 2:3]))
                        after()
                        op(nc.vector.tensor_scalar(PR[st][:, i % 2, 0:nk], PR[st][:, i % 2, 0:nk], STM[:, i % 4, 2:3], None, ALU.mult),
                           scaled.sem, scaled.at(l, st, i))

                    rowmax(i0)
                    rowmax(i0 + 1)
                    rescale(i0)
                    for i in range(i0, n):
                        tt, h = us[i]
                        if i + 1 < n:
                            rescale(i + 1)
                        if i + 2 < n:
                            rowmax(i + 2)
                        name = s[:3] + ("C", i)
                        ready(name)
                        o = 64 * (h % 2)
                        c = (2 if l == 0 else 0) + h // 2
                        taken(nc.vector.tensor_copy(YT[st][o:o + 64, c, tt * P:tt * P + P], bank(name)[o:o + 64, 0:P]), name)
                elif kind == "pool":
                    st = s[1]
                    for a, g in pool_steps():
                        name = s + (a, g)
                        ready(name)
                        if a == "PA":
                            taken(nc.vector.tensor_copy(PL[0:64, g % 2, :], bank(name)[0:64, 0:256]), name)
                        else:
                            o = 64 * (g % 2)
                            taken(nc.vector.tensor_scalar(YT[st][o:o + 64, g // 2, :], bank(name)[o:o + 64, 0:256],
                                                          PS[o:o + 64, g // 2:g // 2 + 1], None, ALU.mult), name)
                elif kind == "out":
                    _, l, st = s
                    dve.wait_ge(*evac(("bc", l, st, G1, 1)))
                    for b in range(D // CW):
                        name = s + (b,)
                        ready(name)
                        y = bank(name).rearrange("p (a n) -> p a n", a=2)
                        g = G1B[:, b * CW:(b + 1) * CW].unsqueeze(1).to_broadcast([P, 2, CW])
                        x = X[:, 2 * st:2 * st + 2, b * CW:(b + 1) * CW]
                        op(nc.vector.tensor_tensor(y, y, g, ALU.mult))
                        after()
                        taken(nc.vector.tensor_tensor(x, x, y, ALU.add), name)
                elif kind == "topk":
                    _, l, tile, hf = s
                    st, tt = tile // 2, tile % 2
                    after()
                    for h in range(4):
                        dve.wait_ge(*evac(("score", l, st, "R", 4 * hf + h)))
                        for side in range(2):
                            topk16(TV[:, side, h, :], TI[:, side, h, :], SC[:, tt, 2 * (4 * hf + h) + side, :])
                    after()
                    op(nc.vector.tensor_scalar(TF[:, 0, :, :], TI[:, 0, :, :], float(NKEYS), float(l * NEXP), ALU.mult, ALU.add),
                       scores_used.sem, scores_used.at(*s))
                    op(nc.vector.tensor_copy(TF[:, 1, :, :], TI[:, 1, :, :]))
                    after()
                    for dst, src in ((CA, TV), (CI, TF)):
                        o = 0
                        for r0, nr, ncol in CAND:
                            out = dst[:, :, o:o + nr * ncol].rearrange("p h (a b) -> p h a b", a=nr)
                            first = src[:, 0, :, r0:r0 + nr].unsqueeze(3).to_broadcast([P, 4, nr, ncol])
                            second = src[:, 1, :, 0:ncol].unsqueeze(2).to_broadcast([P, 4, nr, ncol])
                            op(nc.vector.tensor_tensor(out, first, second, ALU.add))
                            o += nr * ncol
                    after()
                    for h in range(4):
                        topk16(SV[:, h, :], PI[:, h, :], CA[:, h, :])
                    after()
                    op(nc.vector.tensor_copy(SM[:, :], SV[:, :, 0]))
                    after()
                    op(nc.vector.tensor_tensor(SV[:, :, :], SV[:, :, :], SM[:, :].unsqueeze(2).to_broadcast([P, 4, TOPK]), ALU.subtract),
                       shifted.sem, shifted.at(*s))
                    op(nc.vector.tensor_copy(PF[:, :, :], PI[:, :, :]))
                    after()
                    k50 = [P, 4 * TOPK, NCAND]
                    oh3 = OHR[:, :].rearrange("p (k n) -> p k n", n=NCAND)
                    op(nc.vector.tensor_tensor(oh3, PF[:, :, :].rearrange("p h k -> p (h k)").unsqueeze(2).to_broadcast(k50),
                                               IOF[:, :].unsqueeze(1).to_broadcast(k50), ALU.is_equal))
                    after()
                    op(nc.vector.tensor_tensor(OH, OH, CI[:, :, :].unsqueeze(2).to_broadcast([P, 4, TOPK, NCAND]), ALU.mult))
                    after()
                    op(nc.vector.tensor_reduce(out=IF[:, :, :].rearrange("p h k -> p (h k)"), in_=oh3, axis=AX.X, op=ALU.add))
                    after()
                    cols = slice(64 * hf, 64 * hf + 64)
                    op(nc.vector.tensor_copy(IDX[:, tile % 2, cols], IF[:, :, :].rearrange("p h k -> p (h k)")))
                    dve.wait_ge(texp.sem, texp.at(*s))
                    op(nc.vector.tensor_reduce(out=SM[:, :], in_=SV[:, :, :], axis=AX.X, op=ALU.add))
                    after()
                    op(nc.vector.reciprocal(SM[:, :], SM[:, :]))
                    after()
                    op(nc.vector.tensor_tensor(WG[:, tile % 2, cols].rearrange("p (h k) -> p h k", k=TOPK), SV[:, :, :],
                                               SM[:, :].unsqueeze(2).to_broadcast([P, 4, TOPK]), ALU.mult),
                       chosen.sem, chosen.at(*s))
                elif kind == "experts":
                    _, l, tile, part = s
                    if part == "0":
                        after()
                        chunk(l, tile, 0, 0, tile - 1, tile == 0)
                        last[0] = (weighted, chunk0(l, tile) + 1) if tile == 0 else (updated, 2 * chunk0(l, tile))
                    elif part == "loop":
                        after()
                        with dve.Fori(1, PH // 2 - 1) as p:
                            chunk(l, tile, p, 0, tile, False)
                            chunk(l, tile, p, 1, tile, False)
                        last[0] = (updated, 2 * (chunk0(l, tile) + 5))
                    else:
                        h = int(part)
                        chunk(l, tile, h // 2, h % 2, tile, False)
                        last[0] = (updated, 2 * (chunk0(l, tile) + h))
                elif kind == "experts_end":
                    l = s[1]
                    tile = TILES[l][-1]
                    c = chunk0(l, tile) + PH - 1
                    update(c, 1, tile)
                    last[0] = (updated, 2 * c + 2)

        @block.scalar
        def _(act):
            def taken(ins, name):
                ins.then_inc(act_evac, 1)

            def ready(name):
                act.wait_ge(product, work[name] + 1)

            def gelu(c, hh):
                act.wait_ge(dotted, (c + 1) * TOPK)
                nc.scalar.activation(GA[:, hh, :], A[:, hh, :], ACT.Gelu).then_inc(gelud, 1)

            def diags(c, hh):
                act.wait_ge(weighted, c + 1)
                for s in range(TOPK):
                    if not (isinstance(c, int) and c == 0 and s < 4):
                        act.wait_ge(vsum, c * TOPK + s - 3)
                    nc.scalar.activation(DG[:, s % 4, :], ident[:, :], ACT.Copy, scale=WT[:, hh, s:s + 1]).then_inc(diag, 1)

            for s in SCHEDULE:
                kind = s[0]
                if kind == "prep":
                    ready(("rows",))
                    taken(nc.scalar.activation(CT[:, :], bank(("rows",))[:, 0:144], ACT.Copy), ("rows",))
                    act.wait_ge(act_evac, 1)
                    nc.scalar.activation(SE[:, :, :], CT[:, 0:16].rearrange("p (s j) -> p s j", s=2), ACT.Exp,
                                         scale=-1.0).then_inc(exp_c, 1)
                    ready(("keys",))
                    taken(nc.scalar.activation(KT[:, :, :].rearrange("p k n -> p (k n)"), bank(("keys",)), ACT.Copy), ("keys",))
                elif kind == "ada" and s[2] < HALVES:
                    ready(s)
                    taken(nc.scalar.activation(MROW[:, s[2] % 2, :], bank(s)[0:2, :], ACT.Copy), s)
                elif kind in ("norm", "final"):
                    act.wait_ge(sumsq.sem, sumsq.at(*s))
                    nc.scalar.activation(SS[:, :], SS[:, :], ACT.Sqrt, bias=EPT[:, :], scale=1.0 / D).then_inc(sqrted.sem, 1)
                elif kind == "hT":
                    _, l, which, st = s
                    if which == 1:
                        act.wait_ge(*evac(("adaT", l, 3)))
                    for jj in range(KC // 2):
                        name = s + (jj,)
                        ready(name)
                        cols = slice(st * 256, st * 256 + 256)
                        if which == 1:
                            for c in range(2):
                                j = 2 * jj + c
                                ins = nc.scalar.activation(HT[:, j, cols], bank(name)[:, c * 256:c * 256 + 256], ACT.Identity,
                                                           bias=MOD[:, l, SH1 * 8 + j, st:st + 1],
                                                           scale=MOD[:, l, SC1 * 8 + j, st:st + 1])
                        else:
                            ins = nc.scalar.activation(HT[:, 2 * jj:2 * jj + 2, cols],
                                                       bank(name).rearrange("p (c n) -> p c n", c=2), ACT.Copy)
                        taken(ins, name)
                elif kind == "in":
                    _, l, b, streams = s
                    if s == ("in", 0, 1, (CTX,)):
                        act.wait_ge(scores_used.sem, scores_used.at("topk", 0, 0, 1))
                    for st in streams:
                        name = s[:3] + (st,)
                        ready(name)
                        dst = QKVL[:, :, b * CW:(b + 1) * CW] if st == LAT else \
                            {0: UN, 4: KN, 5: VC}[b][:, :, :] if b in (0, 4, 5) else QNC[:, :, (b - 1) * CW:b * CW]
                        taken(nc.scalar.activation(dst, bank(name).rearrange("p (a n) -> p a n", a=2), ACT.Copy), name)
                elif kind == "rope" and s[1] == 0:
                    act.wait_ge(hsumsq.sem, hsumsq.at(*s))
                    nh = {"qk": 16, "q": 12, "k": 4}[s[3]]
                    nc.scalar.activation(HS[:, 0:nh], HS[:, 0:nh], ACT.Sqrt, bias=EPT[:, :], scale=1.0 / HD).then_inc(hsqrt.sem, 1)
                elif kind == "tqk":
                    dst = (QT if s[3] == "q" else KTS)[s[2]]
                    for name, _ in WORK:
                        if name[:4] == s:
                            ready(name)
                            i = name[4]
                            taken(nc.scalar.activation(dst[:, 2 * i:2 * i + 2, :],
                                                       bank(name).rearrange("p (c n) -> p c n", c=2), ACT.Copy), name)
                elif kind == "att":
                    _, l, st, i0, n = s
                    us = units(l, st)
                    nk = 512 if st == LAT else 256

                    def exps(i):
                        name = s[:3] + ("A", i)
                        ready(name)
                        act.wait_ge(maxed.sem, maxed.at(l, st, i))
                        if l == 1:
                            h = us[i][1]
                            nc.scalar.activation(STM[:, i % 4, 3:4], SK[:, h:h + 1], ACT.Exp,
                                                 bias=STM[:, i % 4, 1:2]).then_inc(ach, 1)
                        nc.scalar.activation(PR[st][:, i % 2, 0:nk], bank(name)[:, 0:nk], ACT.Exp, bias=STM[:, i % 4, 1:2],
                                             scale=SCALE, accum_out=STM[:, i % 4, 2:3]).then_inc(expd.sem, 1)

                    exps(i0)
                    exps(i0 + 1)
                    for i in range(i0, n):
                        name = s[:3] + ("B", i)
                        ready(name)
                        taken(nc.scalar.activation(PT[st][:, i % 2, 0:nk], bank(name)[:, 0:nk], ACT.Copy), name)
                        if i + 2 < n:
                            exps(i + 2)
                elif kind == "bc":
                    _, l, st = s
                    if s != ("bc", 0, LAT):
                        prev = ("norm", 0, 2, LAT if l == 0 else CTX)
                        act.wait_ge(normed.sem, normed.at(*prev))
                    for v, dst in ((G1, G1B), (SC2, A2B), (SH2, B2B), (G2, G2B[st])):
                        for hf in range(2):
                            name = s + (v, hf)
                            ready(name)
                            taken(nc.scalar.activation(dst[:, hf * 512:hf * 512 + 512], bank(name), ACT.Copy), name)
                elif kind == "score":
                    _, l, st, heads = s
                    for a, h in score_steps(heads):
                        name = ("score", l, st, a, h)
                        ready(name)
                        if a == "Q":
                            taken(nc.scalar.activation(QS[:, h % 2, :, :], bank(name).rearrange("p (a n) -> p a n", a=2),
                                                       ACT.Copy), name)
                        else:
                            if st == CTX:
                                act.wait_ge(scores_used.sem, scores_used.at("topk", l, 1, h // 4))
                            taken(nc.scalar.activation(SC[:, :, 2 * h:2 * h + 2, :],
                                                       bank(name).rearrange("p (a s n) -> p a s n", a=2, s=2), ACT.Copy), name)
                elif kind == "topk":
                    act.wait_ge(shifted.sem, shifted.at(*s))
                    nc.scalar.activation(SV[:, :, :], SV[:, :, :], ACT.Exp).then_inc(texp.sem, 1)
                elif kind == "experts":
                    _, l, tile, part = s
                    c0 = chunk0(l, tile)
                    if part != "loop":
                        c = c0 + int(part)
                        if c > chunk0(l, 0):
                            diags(c - 1, (c - 1) % 2)
                        gelu(c, c % 2)
                    else:
                        with act.Fori(1, PH // 2 - 1) as p:
                            diags(c0 + 2 * p - 1, 1)
                            gelu(c0 + 2 * p, 0)
                            diags(c0 + 2 * p, 0)
                            gelu(c0 + 2 * p + 1, 1)
                elif kind == "experts_end":
                    diags(chunk0(s[1], TILES[s[1]][-1]) + PH - 1, 1)

        @block.tensor
        def _(pe):
            n_work = [0]

            def begin(name):
                i = work[name]
                assert i == n_work[0], (name, WORK[n_work[0]])
                n_work[0] += 1
                if i >= 4:
                    pe.wait_ge(*evac(WORK[i - 4][0]))
                return bank(name)

            def done(ins):
                ins.then_inc(product, 1)

            def weights(name):
                i = blk[name]
                pe.wait_ge(blk_in[i % WSLOTS], 16 * (i // WSLOTS + 1))
                return WR[:, i % WSLOTS, :, :]

            def tr(out, in_, k=P):
                return nc.tensor.transpose(out, in_, ident[0:k, 0:k])

            def vsums(c, par):
                if not (isinstance(c, int) and c < 2):
                    pe.wait_ge(updated, 2 * c - 2)
                for s in range(TOPK):
                    pe.wait_ge(v_in[s % NV], 16 * (2 * c + s // NV + 1))
                    pe.wait_ge(diag, c * TOPK + s + 1)
                    for hf in range(2):
                        ins = nc.tensor.matmul(acc[:, par, hf * 512:hf * 512 + 512], DG[:, s % 4, :],
                                               V[:, s % NV, hf * 512:hf * 512 + 512],
                                               start=(s == 0), stop=(s == TOPK - 1))
                    ins.then_inc(vsum, 1)

            for s in SCHEDULE:
                kind = s[0]
                if kind == "prep":
                    pe.wait_ge(consts, 6)
                    pe.wait_ge(loaded["rows"], 96)
                    o = begin(("rows",))
                    tr(o[:, 0:96], R1[:, :], 96)
                    done(tr(o[:, 96:144], R2[:, :], 48))
                    pe.wait_ge(loaded["keys"], 64)
                    o = begin(("keys",))
                    for k in range(4):
                        ins = tr(o[:, k * P:k * P + P], KR[:, k, :])
                    done(ins)
                elif kind == "ada":
                    _, l, k = s
                    if k < HALVES:
                        if k == 0:
                            pe.wait_ge(silu_done, 1)
                        o = begin(s)
                        for b in range(2):
                            w = weights(("ada", l, 2 * k + b))
                            for j in range(KC):
                                ins = nc.tensor.matmul(o[0:2, b * CW:(b + 1) * CW], SIL[:, :, j], w[:, j, :],
                                                       start=(j == 0), stop=(j == KC - 1))
                            if b == 0:
                                ins.then_inc(ada_first, 1)
                        done(ins)
                    if k > 0:
                        name = ("adaT", l, k - 1)
                        pe.wait_ge(*evac(("ada", l, k - 1)))
                        o = begin(name)
                        for i in range(4):
                            ins = tr(o[:, 2 * i:2 * i + 2], MROW[:, (k - 1) % 2, i * P:i * P + P], 2)
                        done(ins)
                elif kind == "hT":
                    _, l, which, st = s
                    pe.wait_ge(normed.sem, normed.at("norm", l, which, st))
                    for jj in range(KC // 2):
                        o = begin(s + (jj,))
                        for c in range(2):
                            for tt in range(2):
                                ins = tr(o[:, c * 256 + tt * P:c * 256 + tt * P + P],
                                         H[:, 2 * st + tt, (2 * jj + c) * P:(2 * jj + c + 1) * P])
                        done(ins)
                elif kind == "in":
                    _, l, b, streams = s
                    w = weights(s)
                    for st in streams:
                        pe.wait_ge(*evac(("hT", l, 1, st, KC // 2 - 1)))
                        o = begin(s[:3] + (st,))
                        for tt in range(2):
                            for j in range(KC):
                                ins = nc.tensor.matmul(o[:, tt * CW:(tt + 1) * CW],
                                                       HT[:, j, (2 * st + tt) * P:(2 * st + tt + 1) * P], w[:, j, :],
                                                       start=(j == 0), stop=(j == KC - 1))
                        done(ins)
                elif kind == "tqk":
                    _, l, st, part = s
                    for r_ in ropes:
                        if r_[1] == l and r_[2] // 2 == st and part in r_[3]:
                            pe.wait_ge(roped.sem, roped.at(*r_))
                    if (l, st) == (1, CTX):
                        pe.wait_ge(*evac(("in", l, 4, st)))
                    for name, _ in WORK:
                        if name[:4] == s:
                            o = begin(name)
                            for c in range(2):
                                for tt in range(2):
                                    i = 2 * name[4] + c
                                    cols = slice(c * 256 + tt * P, c * 256 + tt * P + P)
                                    if part == "q":
                                        src = QKVL[:, tt, QOFF[l] + i * P:QOFF[l] + (i + 1) * P] if st == LAT else \
                                            QNC[:, tt, i * P:(i + 1) * P]
                                        ins = tr(o[:, cols], src)
                                    else:
                                        src = QKVL[:, tt, KOFF + i * HD:KOFF + (i + 1) * HD] if st == LAT else \
                                            KN[:, tt, i * HD:(i + 1) * HD]
                                        for q0 in (0, 64):
                                            ins = nc.tensor.matmul(o[q0:q0 + 64, cols], src, ident[:, :],
                                                                   start=True, stop=True)
                            done(ins)
                elif kind == "att":
                    _, l, st, i0, n = s
                    us = units(l, st)
                    group = QH[l] // NKV
                    nk = 512 if st == LAT else 256
                    pe.wait_ge(*evac(("tqk", l, st, "q", QH[l] // 4 - 1)))
                    for stk in (LAT, CTX):
                        pe.wait_ge(*evac(("tqk", l, stk, "k", 1)))
                    pe.wait_ge(*evac(("in", l, 5, CTX)))
                    for a, i in att_steps(i0, n):
                        tt, h = us[i]
                        name = s[:3] + (a, i)
                        if a == "A":
                            o = begin(name)
                            q0 = 64 * (h % 2)
                            masked = l == 1
                            for k0, stk in (((256, CTX), (0, LAT)) if st == LAT else ((0, CTX),)):
                                ins = nc.tensor.matmul(o[:, k0:k0 + 256], QT[st][q0:q0 + 64, h // 2, tt * P:tt * P + P],
                                                       KTS[stk][q0:q0 + 64, h // group, :], start=True,
                                                       stop=not (masked and stk == LAT))
                            if masked:
                                m0 = P * (1 - tt)
                                ins = nc.tensor.matmul(o[:, m0:m0 + P], ident[:, :], MK[:, tt, :], start=False, stop=True)
                        elif a == "B":
                            pe.wait_ge(scaled.sem, scaled.at(l, st, i))
                            o = begin(name)
                            for kc in range(nk // P):
                                ins = tr(o[:, kc * P:kc * P + P], PR[st][:, i % 2, kc * P:kc * P + P])
                        else:
                            pe.wait_ge(*evac(s[:3] + ("B", i)))
                            o = begin(name)
                            q0 = 64 * (h % 2)
                            kv = h // group
                            for kc in range(nk // P):
                                v = QKVL[:, kc, VOFF + kv * HD:VOFF + (kv + 1) * HD] if st == LAT and kc < 2 else \
                                    VC[:, kc % 2, kv * HD:(kv + 1) * HD]
                                ins = nc.tensor.matmul(o[q0:q0 + 64, 0:P], v,
                                                       PT[st][:, i % 2, kc * P:kc * P + P], start=(kc == 0), stop=(kc == nk // P - 1))
                        done(ins)
                elif kind == "pool":
                    st = s[1]
                    pe.wait_ge(loaded["pm"], 16)
                    pe.wait_ge(loaded["small"], 96)
                    pe.wait_ge(*evac(("in", 0, 0, st)))
                    for a, g in pool_steps():
                        name = s + (a, g)
                        if a == "PA":
                            o = begin(name)
                            for tt in range(2):
                                un = (QKVL if st == LAT else UN)[:, tt, g * 64:g * 64 + 64]
                                ins = nc.tensor.matmul(o[0:64, 0:256], un, PM[:, tt, g, :],
                                                       start=(tt == 0), stop=(tt == 1))
                        else:
                            pe.wait_ge(*evac(s + ("PA", g)))
                            o = begin(name)
                            q0 = 64 * (g % 2)
                            ins = nc.tensor.matmul(o[q0:q0 + 64, 0:256], PW[:, g, :], PL[0:64, g % 2, :], start=True, stop=True)
                        done(ins)
                elif kind == "bc":
                    _, l, st = s
                    pe.wait_ge(*evac(("adaT", l, HALVES - 1)))
                    for v in (G1, SC2, SH2, G2):
                        for hf in range(2):
                            o = begin(s + (v, hf))
                            for i in range(4):
                                j = 4 * hf + i
                                ins = nc.tensor.matmul(o[:, i * P:i * P + P],
                                                       MOD[:, l, v * 8 + j, st:st + 1].to_broadcast([P, P]), ident[:, :],
                                                       start=True, stop=True)
                            done(ins)
                elif kind == "out":
                    _, l, st = s
                    pe.wait_ge(*evac(("att", l, st, "C", len(units(l, st)) - 1)))
                    if l == 0:
                        pe.wait_ge(*evac(("pool", st, "PB", 3)))
                    for b in range(D // CW):
                        w = weights(s + (b,))
                        o = begin(s + (b,))
                        for tt in range(2):
                            for j in range(KC):
                                ins = nc.tensor.matmul(o[:, tt * CW:(tt + 1) * CW], YT[st][:, j, tt * P:tt * P + P], w[:, j, :],
                                                       start=(j == 0), stop=(j == KC - 1))
                        done(ins)
                elif kind == "score":
                    _, l, st, heads = s
                    pe.wait_ge(*evac(("hT", l, 2, st, KC // 2 - 1)))
                    for a, h in score_steps(heads):
                        name = ("score", l, st, a, h)
                        if a == "Q":
                            w = weights(("wq", l, st, h))
                            o = begin(name)
                            for half in range(2):
                                for j in range(KC):
                                    ins = nc.tensor.matmul(o[:, half * 256:half * 256 + 256], w[:, j, half * P:half * P + P],
                                                           HT[:, j, st * 256:st * 256 + 256], start=(j == 0), stop=(j == KC - 1))
                            done(ins)
                        else:
                            pe.wait_ge(*evac(("score", l, st, "Q", h)))
                            o = begin(name)
                            for tt in range(2):
                                for half in range(2):
                                    ins = nc.tensor.matmul(o[:, (2 * tt + half) * P:(2 * tt + half + 1) * P],
                                                           QS[:, h % 2, half, tt * P:tt * P + P], KT[:, 2 * l + half, :],
                                                           start=True, stop=True)
                            done(ins)
                elif kind == "experts":
                    _, l, tile, part = s
                    c0 = chunk0(l, tile)
                    if part != "loop":
                        c = c0 + int(part)
                        if c > chunk0(l, 0):
                            vsums(c - 1, (c - 1) % 2)
                    else:
                        with pe.Fori(1, PH // 2 - 1) as p:
                            vsums(c0 + 2 * p - 1, 1)
                            vsums(c0 + 2 * p, 0)
                elif kind == "experts_end":
                    vsums(chunk0(s[1], TILES[s[1]][-1]) + PH - 1, 1)


INPUTS = ["x", "c", "ctx", "c_ctx", "ada_w", "ada_b", "norm1_g", "norm2_g", "final_g", "e_w_in", "e_q_norm_g",
          "e_k_norm_g", "e_pool_w", "e_pool_scale", "e_w_out", "o_w_in", "o_sink", "o_w_out", "p_w_q", "p_keys1",
          "p_keys2", "p_u", "p_v"]


def shape_constants(seq, head_dim):
    import numpy as np
    grid_w, half = 64, head_dim // 2
    pos = np.arange(seq)
    inv = (1.0 / (np.float32(10000.0) ** (np.arange(0, half, 2, dtype=np.float32) / np.float32(half)))).astype(np.float32)
    rope = np.zeros((2, 128, 2, head_dim), np.float32)
    for axis, coord in enumerate((pos // grid_w, pos % grid_w)):
        ang = coord.astype(np.float32)[:, None] * inv[None, :]
        cos, sin = np.cos(ang).astype(np.float32), np.sin(ang).astype(np.float32)
        o = axis * half
        c = np.concatenate([cos, cos], 1).reshape(2, 128, half)
        s = np.concatenate([-sin, sin], 1).reshape(2, 128, half)
        rope[:, :, 0, o:o + half] = c
        rope[:, :, 1, o:o + half] = s
    pm = np.zeros((4, seq, seq), np.float32)
    for g, w in enumerate((2, 4, 8, 16)):
        for q in range(seq):
            lo, hi = max(q - w // 2, 0), min(q + w - w // 2, seq)
            pm[g, lo:hi, q] = np.float32(1.0) / np.float32(hi - lo)
            pm[g, q, q] -= 1.0
    pool = pm.reshape(4, 2, 128, seq).transpose(2, 1, 0, 3)
    return np.ascontiguousarray(rope.transpose(1, 0, 2, 3)), np.ascontiguousarray(pool)


def kernel(**inputs):
    import numpy as np
    import concourse.bacc as bacc
    from concourse.bass_utils import run_bass_kernel_spmd as run

    nc = bacc.Bacc("TRN2", target_bir_lowering=False, num_devices=1)
    arrays, tensors = {}, {}
    rope, pool_m = shape_constants(256, 64)
    for name in INPUTS + ["rope", "pool_m"]:
        a = {"rope": rope, "pool_m": pool_m}[name] if name in ("rope", "pool_m") else np.ascontiguousarray(inputs[name])
        arrays[f"in_{name}"] = a
        tensors[name] = nc.dram_tensor(f"in_{name}", a.shape, mybir.dt.from_np(a.dtype), kind="ExternalInput").ap()
    tensors["out"] = nc.dram_tensor("out_x", (1, 256, 1024), F32, kind="ExternalOutput").ap()
    program(nc, tensors)
    r = run(nc, [arrays], core_ids=[0])
    return r.results[0]["out_x"]
```

```python
from contextlib import ExitStack

import concourse.bass as bass
from concourse import mybir

F32 = mybir.dt.float32
U32 = mybir.dt.uint32
I32 = mybir.dt.int32
ALU = mybir.AluOpType
ACT = mybir.ActivationFunctionType
AX = mybir.AxisListType

P = 128
D = 1024
KC = D // P
DEPTH = 2
LAT, CTX = 0, 1
HD = 64
NKV = 4
QH = (12, 16)
QOFF = (256, 0)
KOFF, VOFF, DIN = 1024, 1280, 1536
CW = 256
WSLOTS = 3
EARLY_ROWS = (3, 5, 7, 10, 12, 14)
LATE_SLOTS = (4, 5, 3)
LATE_HEADS = (3, 4, 5)
EPS = 1e-6
PH = 8
TOPK = 16
NKEYS = 128
NEXP = NKEYS * NKEYS
NU = NV = 8
PAIR = 2 * TOPK
CAND = [(0, 1, 16), (1, 1, 8), (2, 1, 5), (3, 1, 4), (4, 1, 3), (5, 3, 2), (8, 8, 1)]
NCAND = sum(r * c for _, r, c in CAND)
SCALE = HD ** -0.5
LOWEST = -3.0e38
MASKED = -1e30 / SCALE
SH1, SC1, G1, SH2, SC2, G2 = range(6)
HALVES = 12
TILES = ((0, 1, 2, 3), (0, 1))


def gather_stages(l, between):
    s = []
    for t in TILES[l]:
        for part in ("0", "1", "loop", "6", "7"):
            s += [("experts", l, t, part)] + between.get((t, part), [])
    return s + [("experts_end", l)]


def schedule():
    both = (LAT, CTX)
    s = [("prep",)] + [("ada", 0, k) for k in range(5)]
    s += [("norm", 0, 1, LAT), ("norm", 0, 1, CTX), ("tables",), ("hT", 0, 1, LAT), ("hT", 0, 1, CTX)]
    s += [("in", 0, 4, both), ("ada", 0, 5), ("in", 0, 1, (LAT,)), ("ada", 0, 6), ("in", 0, 2, (LAT,)), ("ada", 0, 7),
          ("in", 0, 3, (LAT,)), ("ada", 0, 8), ("rope", 0, 0, "qk"), ("in", 0, 5, both), ("ada", 0, 9),
          ("rope", 0, 1, "qk"), ("in", 0, 0, both), ("rope", 0, 2, "k"), ("rope", 0, 3, "k"), ("pool", LAT), ("pool", CTX)]
    s += [("ada", 0, k) for k in range(10, HALVES + 1)]
    s += [("tqk", 0, LAT, "q"), ("tqk", 0, LAT, "k"), ("tqk", 0, CTX, "k"), ("att", 0, LAT, 0, 12)]
    s += [("bc", 0, LAT, (G1,)), ("out", 0, LAT), ("norm", 0, 2, LAT), ("hT", 0, 2, LAT), ("bc", 0, LAT, (SC2, SH2)),
          ("rows", 0, LAT)]
    s += [("score", 0, LAT, (0, 1)), ("topk", 0, 0, 0), ("bc", 0, LAT, (G2,)), ("score", 0, LAT, (2, 3)), ("score", 0, LAT, (4,)),
          ("topk", 0, 0, 1), ("score", 0, LAT, (5, 6, 7))]
    s += gather_stages(0, {
        (0, "0"): [("topk", 0, 0, 2)],
        (0, "1"): [("topk", 0, 0, 3), ("topk", 0, 1, 0)],
        (0, "loop"): [("topk", 0, 1, 1), ("in", 0, 1, (CTX,)), ("in", 0, 2, (CTX,)), ("in", 0, 3, (CTX,)),
                      ("rope", 0, 2, "q"), ("rope", 0, 3, "q")],
        (0, "6"): [("tqk", 0, CTX, "q"), ("att", 0, CTX, 0, 4)],
        (0, "7"): [("att", 0, CTX, 4, 8)],
        (1, "0"): [("att", 0, CTX, 8, 12)],
        (1, "1"): [("bc", 0, CTX, (G1, SC2, SH2, G2)), ("topk", 0, 1, 2), ("topk", 0, 1, 3), ("out", 0, CTX)],
        (1, "loop"): [("norm", 0, 2, CTX), ("hT", 0, 2, CTX), ("rows", 0, CTX), ("score", 0, CTX, (0, 1))],
        (1, "6"): [("topk", 0, 2, 0), ("score", 0, CTX, (2, 3))],
        (1, "7"): [("topk", 0, 2, 1), ("score", 0, CTX, (4, 5))],
        (2, "0"): [("topk", 0, 2, 2), ("score", 0, CTX, (6, 7)), ("ada", 1, 0)],
        (2, "1"): [("topk", 0, 2, 3), ("ada", 1, 1), ("ada", 1, 2)],
        (2, "loop"): [("ada", 1, 3), ("ada", 1, 4), ("norm", 1, 1, LAT)],
        (2, "6"): [("topk", 0, 3, 0), ("hT", 1, 1, LAT), ("in", 1, 0, (LAT,)), ("in", 1, 1, (LAT,))],
        (2, "7"): [("topk", 0, 3, 1), ("in", 1, 2, (LAT,)), ("ada", 1, 5)],
        (3, "0"): [("topk", 0, 3, 2), ("in", 1, 3, (LAT,)), ("ada", 1, 6)],
        (3, "1"): [("topk", 0, 3, 3), ("in", 1, 4, (LAT,)), ("ada", 1, 7)],
        (3, "loop"): [("in", 1, 5, (LAT,)), ("rope", 1, 0, "qk"), ("rope", 1, 1, "qk"), ("ada", 1, 8), ("ada", 1, 9)],
        (3, "6"): [("tqk", 1, LAT, "q"), ("tqk", 1, LAT, "k"), ("ada", 1, 10), ("ada", 1, 11), ("ada", 1, 12)],
    })
    s += [("norm", 1, 1, CTX), ("hT", 1, 1, CTX), ("in", 1, 4, (CTX,)), ("in", 1, 5, (CTX,)), ("tqk", 1, CTX, "k")]
    s += [("att", 1, LAT, 0, 16), ("bc", 1, LAT, (G1,)), ("out", 1, LAT), ("norm", 1, 2, LAT), ("hT", 1, 2, LAT),
          ("bc", 1, LAT, (SC2, SH2)), ("rows", 1, LAT)]
    s += [("score", 1, LAT, (0, 1)), ("topk", 1, 0, 0), ("bc", 1, LAT, (G2,)), ("score", 1, LAT, (2, 3)), ("score", 1, LAT, (4,)),
          ("topk", 1, 0, 1), ("score", 1, LAT, (5, 6, 7))]
    s += gather_stages(1, {
        (0, "0"): [("topk", 1, 0, 2)],
        (0, "1"): [("topk", 1, 0, 3)],
        (0, "6"): [("topk", 1, 1, 0)], (0, "7"): [("topk", 1, 1, 1)],
        (1, "0"): [("topk", 1, 1, 2)], (1, "1"): [("topk", 1, 1, 3)]})
    return s + [("final",)]


SCHEDULE = schedule()


def units(l):
    return [(tt, h) for tt in range(2) for h in range(0, QH[l], 2)]


def score_steps(heads):
    steps = [("Q", heads[0])]
    for i, h in enumerate(heads):
        if i + 1 < len(heads):
            steps.append(("Q", heads[i + 1]))
        steps.append(("R", h))
    return steps


def att_steps(lo, n):
    steps = [("A", lo), ("A", lo + 1)]
    for i in range(lo, n):
        steps.append(("B", i))
        if i + 2 < n:
            steps.append(("A", i + 2))
        if i > lo:
            steps.append(("C", i - 1))
    return steps + [("C", n - 1)]


def pool_steps():
    return [("PA", 0), ("PA", 1), ("PB", 0), ("PA", 2), ("PB", 1), ("PA", 3), ("PB", 2), ("PB", 3)]


def work_order():
    w = []
    for s in SCHEDULE:
        k = s[0]
        if k == "prep":
            w += [(("rows",), "act"), (("keys",), "act")]
        elif k == "ada":
            if s[2] < HALVES:
                w += [(("ada", s[1], s[2]), "act")]
            if s[2] > 0:
                w += [(("adaT", s[1], s[2] - 1), "dve")]
        elif k == "hT":
            w += [(s + (jj,), "act") for jj in range(KC // 2)]
        elif k == "in":
            w += [(s[:3] + (st,), "act") for st in s[3]]
        elif k == "tqk":
            w += [(s + (i,), "act") for i in range(QH[s[1]] // 4 if s[3] == "q" else NKV // 2)]
        elif k == "att":
            w += [(s[:3] + (a, i), {"A": "exp", "B": "act", "C": "dve"}[a]) for a, i in att_steps(s[3], s[4])]
        elif k == "pool":
            w += [(s + (a, g), "act") for a, g in pool_steps()]
        elif k == "bc":
            w += [(s[:3] + (v, hf), "act") for v in s[3] for hf in range(2)]
        elif k == "out":
            w += [(s + (b,), "dve") for b in range(D // CW)]
        elif k == "score":
            w += [(s[:3] + (a, h), "act") for a, h in score_steps(s[3])]
    return w


WORK = work_order()


def work_banks():
    banks, before, user, turn = {}, {}, {}, 0
    for name, _ in WORK:
        if name[0] == "att":
            st, a, i = name[2:]
            b = {"A": (), "B": (0, 1), "C": (2 + i % 2,)}[a] if st == LAT else {"A": (0, 1), "B": (2,), "C": (3,)}[a]
        else:
            b, turn = (turn,), (turn + 1) % 4
        banks[name] = b
        before[name] = sorted({user[x] for x in b if x in user}, key=str)
        user.update({x: name for x in b})
    return banks, before


BANKS, BEFORE = work_banks()


def block_order():
    o = []
    for s in SCHEDULE:
        if s[0] == "ada" and s[2] < HALVES:
            o += [("ada", s[1], 2 * s[2] + i) for i in range(2)]
        elif s[0] == "in":
            o += [s]
        elif s[0] == "out":
            o += [s + (b,) for b in range(D // CW)]
        elif s[0] == "score":
            o += [("wq", s[1], s[2], h) for h in s[3]]
    return o


BLOCKS = block_order()


def block_slots():
    early = BLOCKS.index(("wq", 0, LAT, 0))
    slots, users, turn = [], {}, 0
    for i, name in enumerate(BLOCKS):
        if i < early:
            slot = i % (WSLOTS + len(EARLY_ROWS))
        elif name[0] == "wq" and name[2] == LAT and name[3] in LATE_HEADS:
            slot = WSLOTS + LATE_SLOTS[LATE_HEADS.index(name[3])]
        else:
            slot, turn = turn % WSLOTS, turn + 1
        u = users.setdefault(slot, [])
        slots.append((slot, len(u) + 1, u[-1] if u else None))
        u.append(name)
    return slots


SLOTS = block_slots()


class Count:

    def __init__(self, sem, names):
        self.sem, self.pos = sem, {n: i + 1 for i, n in enumerate(names)}

    def at(self, *name):
        return self.pos[name]


def named(*kinds):
    return [s for s in SCHEDULE if s[0] in kinds]


def program(nc, t):
    x_d, c_d, ctx_d, cctx_d = t["x"], t["c"], t["ctx"], t["c_ctx"]
    out_d = t["out"]
    es = ExitStack()
    with es:
        def sb(name, shape, dt=F32):
            return es.enter_context(nc.sbuf_tensor(name, shape, dt))

        def sem(name):
            return es.enter_context(nc.semaphore(name))

        X = sb("X", [P, 4, D])
        H = sb("H", [P, 4, D])
        HT = sb("HT", [P, KC, 4 * P])
        BC = sb("BC", [P, 5, D])
        G1B, A2B, B2B, G2B = BC[:, 0, :], BC[:, 1, :], BC[:, 2, :], (BC[:, 3, :], BC[:, 4, :])
        WR = sb("WR", [P, WSLOTS, KC, CW])
        RING = sb("RING", [P, NU + NV, D])
        U, V = RING[:, 0:NU, :], RING[:, NU:NU + NV, :]
        QKVL = BC[:, 0:3, :].rearrange("p a b -> p (a b)").rearrange("p (t n) -> p t n", t=2)
        UN = RING[:, 2, 0:512].rearrange("p (t n) -> p t n", t=2)
        KN = RING[:, 2, 512:1024].rearrange("p (t n) -> p t n", t=2)
        VC = sb("VC", [P, 2, CW])
        QT = (H[:, 0:2, :].rearrange("p a b -> p (a b)").rearrange("p (c n) -> p c n", c=8), HT[:, :, 0:256])
        KTS = [G2B[st].rearrange("p (c n) -> p c n", c=NKV) for st in (LAT, CTX)]
        YT = [r_.rearrange("p a b -> p (a b)").rearrange("p (c n) -> p c n", c=8) for r_ in (RING[:, 0:2, :], H[:, 2:4, :])]
        SCR = sb("SCR", [P, 4096])
        SC = SCR[:, :].rearrange("p (t s n) -> p t s n", t=2, s=16)
        QNC = SCR[:, 0:1536].rearrange("p (t n) -> p t n", t=2)
        PR = [m.rearrange("p (r h n) -> p r h n", r=2, h=2) for m in (SCR[:, 0:2048], A2B)]
        PT = [m.rearrange("p (r h n) -> p r h n", r=2, h=2) for m in (SCR[:, 2048:4096], B2B)]
        PM = SCR[:, 2048:4096].rearrange("p (i g n) -> p i g n", i=2, g=4)
        OHR = sb("OHR", [P, 3072])
        OH3 = OHR[:, 0:2 * TOPK * NCAND].rearrange("p (k n) -> p k n", n=NCAND)
        OH = OH3.rearrange("p (h k) n -> p h k n", h=2)
        T1, T2 = OHR[:, 0:1280], OHR[:, 1280:2560]
        PL = OHR[:, 2560:3072].rearrange("p (r n) -> p r n", r=2)
        R1 = H[0:96, 0, 512:640]
        R2 = H[0:48, 0, 640:768]
        CT = sb("CT", [P, 144])
        KR = H[:, 0, 0:512].rearrange("p (k n) -> p k n", k=4)
        KT = sb("KT", [P, 4, P])
        SIL = sb("SIL", [P, KC, 32])
        SEL = sb("SEL", [P, 2])
        SE = sb("SE", [P, 2, KC])
        MOD = sb("MOD", [P, DEPTH, 48, 2])
        RC = sb("RC", [P, 2, 2, HD])
        GN = sb("GN", [P, 2, HD])
        CG = RING[:, 9, 0:512].rearrange("p (t q c n) -> p t q c n", t=2, q=2, c=2)
        PW = RING[0:HD, 9, 512:768].rearrange("p (g n) -> p g n", g=4)
        SK = sb("SK", [P, 16])
        PS = sb("PS", [P, 2])
        ident = sb("ident", [P, P])
        MK = sb("MK", [P, 2, P])
        EPT = sb("EPT", [P, 1])
        SS = sb("SS", [P, 2])
        RS = sb("RS", [P, 2])
        HS = sb("HS", [P, 16])
        HR = sb("HR", [P, 16])
        STM = sb("STM", [P, 4, 4, 2])
        QS = sb("QS", [P, 2, 2, 2 * P])
        MROW = QS[:, :, :, :].rearrange("p r a n -> p r (a n)")
        TV = sb("TV", [P, 2, 2, TOPK])
        TI = sb("TI", [P, 2, 2, TOPK], U32)
        TF = sb("TF", [P, 2, 2, TOPK])
        CA = sb("CA", [P, 2, NCAND])
        CI = sb("CI", [P, 2, NCAND])
        SV = sb("SV", [P, 2, TOPK])
        PI = sb("PI", [P, 2, TOPK], U32)
        PF = sb("PF", [P, 2, TOPK])
        IF = sb("IF", [P, 2, TOPK])
        SM = sb("SM", [P, 2])
        IOI = sb("IOI", [P, NCAND], I32)
        IOF = sb("IOF", [P, NCAND])
        IDX = sb("IDX", [P, 2, PH * TOPK], U32)
        WG = sb("WG", [P, 2, PH * TOPK])
        IU = sb("IU", [P, 2, TOPK], U32)
        IV = sb("IV", [P, 2, TOPK], U32)
        A = sb("A", [P, 2, TOPK])
        GA = sb("GA", [P, 2, TOPK])
        WT = sb("WT", [P, 2, TOPK])
        DG = sb("DG", [P, 4, P])
        acc = es.enter_context(nc.psum_tensor("acc", [P, 2, D], F32))
        wk = es.enter_context(nc.psum_tensor("wk", [P, 4, 512], F32))

        loaded = {n: sem("ld_" + n) for n in ("rows", "keys", "x", "ctx", "small", "pm")}
        final_gain = sem("final_gain")
        blk_in = [sem(f"blk{i}") for i in range(WSLOTS + len(EARLY_ROWS))]
        ada_first = sem("ada_first")
        product = sem("product")
        act_evac, dve_evac = sem("act_evac"), sem("dve_evac")
        consts = sem("consts")
        exp_c, silu_done = sem("exp_c"), sem("silu_done")
        norms = [s for s in SCHEDULE if s[0] in ("norm", "final")]
        sumsq = Count(sem("sumsq"), norms)
        sqrted = Count(sem("sqrted"), norms)
        normed = Count(sem("normed"), norms)
        modulated = Count(sem("modulated"), named("rows"))
        ropes = named("rope")
        hsumsq = Count(sem("hsumsq"), [s for s in ropes if s[1] == 0])
        hsqrt = Count(sem("hsqrt"), [s for s in ropes if s[1] == 0])
        roped = Count(sem("roped"), ropes)
        all_units = [(s[1], s[2], i) for s in named("att") for i in range(s[3], s[4])]
        maxed = Count(sem("maxed"), all_units)
        expd = Count(sem("expd"), all_units)
        scaled = Count(sem("scaled"), all_units)
        topks = named("topk")
        shifted = Count(sem("shifted"), topks)
        texp = Count(sem("texp"), topks)
        chosen = Count(sem("chosen"), topks)
        scores_used = Count(sem("scores_used"), topks)
        u_in = [sem(f"u_in{i}") for i in range(NU)]
        v_in = [sem(f"v_in{i}") for i in range(NV)]
        ixcopy, issued, gate_sem = sem("ixcopy"), sem("issued"), sem("gate_sem")
        dotted, gelud, weighted, diag, vsum, updated = (sem(n) for n in (
            "dotted", "gelud", "weighted", "diag", "vsum", "updated"))
        dch, ach = sem("dch"), sem("ach")
        stored = sem("stored")

        work = {n: i for i, (n, _) in enumerate(WORK)}

        def evac(name):
            i = work[name]
            e = WORK[i][1]
            if e == "exp":
                return expd.sem, expd.at(name[1], name[2], name[4])
            return (act_evac if e == "act" else dve_evac), sum(1 for _, x in WORK[:i + 1] if x == e)

        def bank(name):
            return wk[:, BANKS[name][0], :]

        def att_scores(name):
            st, i = name[2], name[4]
            if st == LAT:
                return acc[:, i % 2, :].rearrange("p (h n) -> p h n", h=2)
            return wk[:, 0:2, (i % 2) * 256:(i % 2) * 256 + 256]

        def att_turned(name):
            if name[2] == LAT:
                return wk[:, 0:2, :]
            return wk[:, 2, :].rearrange("p (h n) -> p h n", h=2)

        blk = {n: i for i, n in enumerate(BLOCKS)}

        def slot_rows(slot):
            if slot < WSLOTS:
                return WR[:, slot, :, :]
            r = EARLY_ROWS[slot - WSLOTS]
            return RING[:, r:r + 2, :].rearrange("p a b -> p (a b)").rearrange("p (k n) -> p k n", k=KC)

        def block_used(name):
            kind, l, b = name[0], name[1], name[2] if name[0] == "in" else name[-1]
            if kind == "ada" and b % 2 == 0:
                return ada_first, HALVES * l + b // 2 + 1
            last = ("ada", l, b // 2) if kind == "ada" else name[:3] + name[3][-1:] if kind == "in" else \
                ("score",) + name[1:3] + ("Q", b) if kind == "wq" else name
            return product, work[last] + 1

        def chunk0(l, t):
            return 32 * l + PH * t

        block = es.enter_context(nc.Block())

        @block.sync
        def _(sp):
            rows = [(R1[0:8], c_d.rearrange("o (j p) -> (o j) p", p=P)),
                    (R1[8:16], cctx_d.rearrange("(j p) -> j p", p=P)),
                    (R1[16:32], t["norm1_g"].rearrange("l (j p) -> (l j) p", p=P)),
                    (R1[32:48], t["norm2_g"].rearrange("l (j p) -> (l j) p", p=P)),
                    (R1[48:96], t["ada_b"][0].rearrange("(j p) -> j p", p=P)),
                    (R2[:, :], t["ada_b"][1].rearrange("(j p) -> j p", p=P))]
            for dst, src in rows:
                sp.dma_start(dst, src).then_inc(loaded["rows"], 16)
            for l in range(DEPTH):
                sp.dma_start(KR[:, 2 * l, :], t["p_keys1"][l]).then_inc(loaded["keys"], 16)
                sp.dma_start(KR[:, 2 * l + 1, :], t["p_keys2"][l]).then_inc(loaded["keys"], 16)
            srcs = {"ada": t["ada_w"], "out": (t["e_w_out"], t["o_w_out"]), "in": (t["e_w_in"], t["o_w_in"]),
                    "wq": t["p_w_q"]}
            for i, name in enumerate(BLOCKS):
                slot, _, before = SLOTS[i]
                if i == 5:
                    sp.dma_start(X[:, 0:2, :], x_d[0].rearrange("(a p) d -> p a d", p=P)).then_inc(loaded["x"], 16)
                if i == 8:
                    sp.dma_start(X[:, 2:4, :], ctx_d[0].rearrange("(a p) d -> p a d", p=P)).then_inc(loaded["ctx"], 16)
                    sp.dma_start(RC[:, :, :, :], t["rope"]).then_inc(loaded["small"], 16)
                    sp.dma_start(GN[:, 0, :], t["e_q_norm_g"].partition_broadcast(P)[:, 0, :]).then_inc(loaded["small"], 16)
                    sp.dma_start(GN[:, 1, :], t["e_k_norm_g"].partition_broadcast(P)[:, 0, :]).then_inc(loaded["small"], 16)
                    sp.dma_start(SK[:, :], t["o_sink"].partition_broadcast(P)[:, 0, :]).then_inc(loaded["small"], 16)
                    sp.dma_start(PW[:, :, :], t["e_pool_w"][0].rearrange("g c d -> c g d")).then_inc(loaded["small"], 16)
                    with nc.allow_non_contiguous_dma(reason="256 words"):
                        sp.dma_start(PS[:, :], t["e_pool_scale"][0].rearrange("(j p) -> p j", p=P)).then_inc(loaded["small"], 16)
                if i == 18:
                    sp.dma_start(PM[:, :, :, :], t["pool_m"]).then_inc(loaded["pm"], 16)
                if name == ("wq", 1, LAT, LATE_HEADS[0]):
                    sp.wait_ge(vsum, chunk0(1, 0) * TOPK)
                if before:
                    sp.wait_ge(*block_used(before))
                kind, l, b = name[0], name[1], name[2] if name[0] == "in" else name[-1]
                w = srcs[kind][0] if (kind in ("in", "out") and l == 0) else \
                    srcs[kind][1] if kind in ("in", "out") else srcs[kind][l]
                if kind in ("in", "out"):
                    w = w[0]
                sp.dma_start(slot_rows(slot), w.rearrange("(j p) n -> p j n", p=P)[:, :, b * CW:(b + 1) * CW]).then_inc(blk_in[slot], 16)
            sp.wait_ge(normed.sem, normed.at("norm", 1, 2, LAT))
            sp.wait_ge(*evac(("out", 1, LAT, D // CW - 1)))
            sp.dma_start(G1B, t["final_g"].partition_broadcast(P)).then_inc(final_gain, 16)
            sp.wait_ge(normed.sem, normed.at("final"))
            sp.dma_start(out_d[0].rearrange("(a p) d -> p a d", p=P), H[:, 0:2, :]).then_inc(stored, 16)
            sp.wait_ge(stored, 16)

        @block.gpsimd
        def _(pool):
            nc.gpsimd.memset(ident[:, :], 0.0).then_inc(consts, 1)
            nc.gpsimd.memset(MK[:, :, :], 0.0).then_inc(consts, 1)
            pool.wait_ge(consts, 2)
            nc.gpsimd.affine_select(out=ident[:, :], in_=ident[:, :], compare_op=ALU.not_equal, fill=1.0,
                                    base=0, pattern=[[-1, P]], channel_multiplier=1).then_inc(consts, 1)
            nc.gpsimd.affine_select(out=MK[:, 0, :], in_=MK[:, 0, :], compare_op=ALU.is_ge, fill=MASKED,
                                    base=0, pattern=[[-1, P]], channel_multiplier=1).then_inc(consts, 1)
            nc.gpsimd.affine_select(out=MK[:, 1, :], in_=MK[:, 1, :], compare_op=ALU.is_ge, fill=MASKED,
                                    base=0, pattern=[[1, P]], channel_multiplier=-1).then_inc(consts, 1)
            nc.gpsimd.iota(IOI[:, :], pattern=[[1, NCAND]], base=0, channel_multiplier=0).then_inc(consts, 1)
            tables = {"u": t["p_u"].rearrange("l n d -> (l n) d"), "v": t["p_v"].rearrange("l n d -> (l n) d")}

            def gate(s, value):
                pool.wait_ge(s, value)
                pool.sem_inc(gate_sem, 1)

            def copy_rows(dst, tile, col):
                nc.gpsimd.tensor_copy(dst, IDX[:, tile % 2, col]).then_inc(ixcopy, 1)

            def gather(table, ring, n, rows, slot_in):
                pool.indirect_dma_start(out=ring[:, n % NU, :], out_offset=None, in_=tables[table],
                                        in_offset=bass.IndirectOffsetOnAxis(ap=rows, axis=0),
                                        engine_sem=issued).then_inc(slot_in[n % NU], 16)

            def chunk(l, tile, p, hh, vtile, vcol, first):
                c = chunk0(l, tile) + 2 * p + hh
                start = first and hh == 0 and tile == 0
                static = isinstance(p, int)
                if not (static and c < 2):
                    gate(issued, 32 * c - 48)
                col = (2 * p + hh) * TOPK
                copy_rows(IU[:, hh, :], tile, slice(col, col + TOPK) if static else bass.ds(col, TOPK))
                if not start:
                    copy_rows(IV[:, 1 - hh, :], vtile, vcol)
                gate(ixcopy, 2 * c + 1)
                for s in range(TOPK):
                    if not (static and c == 0 and s < NU):
                        gate(dotted, c * TOPK + s - NU + 1)
                    gather("u", U, s, IU[:, hh, s:s + 1], u_in)
                    if not start:
                        if not (static and c == 1 and s < NV):
                            gate(vsum, (c - 1) * TOPK + s - NV + 1)
                        gather("v", V, s, IV[:, 1 - hh, s:s + 1], v_in)

            for s in SCHEDULE:
                if s[0] == "experts":
                    _, l, tile, part = s
                    if part == "0":
                        pool.wait_ge(chosen.sem, chosen.at("topk", l, tile, 0))
                        chunk(l, tile, 0, 0, tile - 1, slice(7 * TOPK, 8 * TOPK), True)
                    elif part == "loop":
                        with pool.Fori(1, PH // 2 - 1) as p:
                            gate(chosen.sem, chosen.at("topk", l, tile, 1) - 1 + p)
                            chunk(l, tile, p, 0, tile, bass.ds((2 * p - 1) * TOPK, TOPK), False)
                            chunk(l, tile, p, 1, tile, bass.ds(2 * p * TOPK, TOPK), False)
                    else:
                        h = int(part)
                        pool.wait_ge(chosen.sem, chosen.at("topk", l, tile, h // 2))
                        if tile == 0 and h == 1:
                            pool.wait_ge(product, work[("score", l, LAT, "Q", LATE_HEADS[-1])] + 1)
                        chunk(l, tile, h // 2, h % 2, tile, slice((h - 1) * TOPK, h * TOPK), False)
                elif s[0] == "experts_end":
                    l = s[1]
                    tile = TILES[l][-1]
                    c = chunk0(l, tile) + PH
                    pool.wait_ge(issued, 32 * c - 48)
                    copy_rows(IV[:, 1, :], tile, slice(7 * TOPK, 8 * TOPK))
                    pool.wait_ge(ixcopy, 2 * c)
                    for s_ in range(TOPK):
                        pool.wait_ge(vsum, (c - 1) * TOPK + s_ - NV + 1)
                        gather("v", V, s_, IV[:, 1, s_:s_ + 1], v_in)

        @block.vector
        def _(dve):
            last = [None, 0]

            def op(ins, s=None, value=None):
                if s is None:
                    last[1] += 1
                    ins.then_inc(dch, 1)
                    last[0] = (dch, last[1])
                else:
                    ins.then_inc(s, 1)
                    last[0] = (s, value)

            def after():
                dve.wait_ge(*last[0])

            def taken(ins, name):
                op(ins, *evac(name))

            def ready(name):
                dve.wait_ge(product, work[name] + 1)

            def topk16(lists):
                for h in (0, 8):
                    for vals, _, rows in lists:
                        op(nc.vector.max(out=vals[:, h:h + 8], in_=rows))
                    after()
                    for vals, idxs, rows in lists:
                        op(nc.vector.max_index(out=idxs[:, h:h + 8], in_max=vals[:, h:h + 8], in_values=rows))
                    after()
                    if h == 0:
                        for vals, _, rows in lists:
                            op(nc.vector.match_replace(out=rows, in_to_replace=vals[:, 0:8], in_values=rows, imm_value=LOWEST))
                        after()

            def dots(c, hh, tile):
                for s in range(TOPK):
                    dve.wait_ge(u_in[s % NU], 16 * (2 * c + s // NU + 1))
                    nc.vector.scalar_tensor_tensor(out=U[:, s % NU, :], in0=U[:, s % NU, :], scalar=1.0,
                                                   in1=H[:, tile, :], op0=ALU.mult, op1=ALU.mult,
                                                   accum_out=A[:, hh, s:s + 1]).then_inc(dotted, 1)

            def update(c, par, tile):
                g2 = G2B[tile // 2]
                dve.wait_ge(vsum, (c + 1) * TOPK)
                nc.vector.tensor_tensor(acc[:, par, :], acc[:, par, :], g2, ALU.mult).then_inc(updated, 1)
                dve.wait_ge(updated, 2 * c + 1)
                nc.vector.tensor_tensor(X[:, tile, :], X[:, tile, :], acc[:, par, :], ALU.add).then_inc(updated, 1)

            def chunk(l, tile, p, hh, vtile, start):
                c = chunk0(l, tile) + 2 * p + hh
                dots(c, hh, tile)
                dve.wait_ge(gelud, c + 1)
                col = (2 * p + hh) * TOPK
                g = WG[:, tile % 2, col:col + TOPK] if isinstance(p, int) else WG[:, tile % 2, bass.ds(col, TOPK)]
                nc.vector.tensor_tensor(WT[:, hh, :], GA[:, hh, :], g, ALU.mult).then_inc(weighted, 1)
                if not start:
                    update(c - 1, 1 - hh, vtile)

            for s in SCHEDULE:
                kind = s[0]
                if kind == "prep":
                    op(nc.vector.memset(EPT[:, :], EPS))
                    op(nc.vector.memset(SIL[:, :, :], 0.0))
                    dve.wait_ge(consts, 6)
                    op(nc.vector.tensor_copy(IOF[:, :], IOI[:, :]))
                    op(nc.vector.tensor_reduce(out=SEL[:, :], in_=ident[:, :].rearrange("p (g s) -> p s g", g=4)[:, 0:2, :],
                                               axis=AX.X, op=ALU.add))
                    dve.wait_ge(exp_c, 1)
                    op(nc.vector.tensor_scalar_add(SE[:, :, :], SE[:, :, :], 1.0))
                    after()
                    op(nc.vector.reciprocal(SE[:, :, :], SE[:, :, :]))
                    after()
                    op(nc.vector.tensor_tensor(SIL[:, :, 0:2].rearrange("p j s -> p s j"), SE[:, :, :],
                                               CT[:, 0:16].rearrange("p (s j) -> p s j", s=2), ALU.mult), silu_done, 1)
                elif kind == "tables":
                    dve.wait_ge(loaded["small"], 96)
                    for tt in range(2):
                        cosb = RC[:, tt, 0, :].unsqueeze(1).to_broadcast([P, 2, HD])
                        op(nc.vector.tensor_tensor(CG[:, tt, :, 0, :], GN[:, :, :], cosb, ALU.mult))
                        for a in range(2):
                            for q in range(2):
                                o = CG[:, tt, q, 1, :].rearrange("p (h a n) -> p h a n", h=2, a=2)[:, :, a, :]
                                sn = RC[:, tt, 1, :].rearrange("p (h a n) -> p h a n", h=2, a=2)[:, :, a, :]
                                g = GN[:, q, :].rearrange("p (h a n) -> p h a n", h=2, a=2)[:, :, 1 - a, :]
                                op(nc.vector.tensor_tensor(o, sn, g, ALU.mult))
                elif kind == "ada" and s[2] > 0:
                    l, k = s[1], s[2] - 1
                    name = ("adaT", l, k)
                    ready(name)
                    cols = MOD[:, l, 4 * k:4 * k + 4, :]
                    bias = CT[:, 48 + 48 * l + 4 * k:48 + 48 * l + 4 * k + 4].unsqueeze(2).to_broadcast([P, 4, 2])
                    add = nc.vector.tensor_tensor(cols, bank(name)[:, 0:8].rearrange("p (k s) -> p k s", s=2), bias, ALU.add)
                    if k // 2 in (SC1, SC2):
                        op(add)
                        after()
                        g0 = (16 if k // 2 == SC1 else 32) + 8 * l + 4 * (k % 2)
                        gain = CT[:, g0:g0 + 4].unsqueeze(2).to_broadcast([P, 4, 2])
                        taken(nc.vector.scalar_tensor_tensor(out=cols, in0=cols, scalar=1.0, in1=gain,
                                                             op0=ALU.add, op1=ALU.mult), name)
                    else:
                        taken(add, name)
                elif kind in ("norm", "final"):
                    st = s[3] if kind == "norm" else LAT
                    if s == ("norm", 0, 1, LAT):
                        dve.wait_ge(loaded["x"], 16)
                        dve.wait_ge(*evac(("keys",)))
                    if s == ("norm", 0, 1, CTX):
                        dve.wait_ge(loaded["ctx"], 16)
                    if last[0] is not None:
                        after()
                    for tt in range(2):
                        ins = nc.vector.scalar_tensor_tensor(
                            out=H[:, 2 * st + tt, :], in0=X[:, 2 * st + tt, :], scalar=1.0, in1=X[:, 2 * st + tt, :],
                            op0=ALU.mult, op1=ALU.mult, accum_out=SS[:, tt:tt + 1])
                        if tt == 0:
                            op(ins)
                    op(ins, sumsq.sem, sumsq.at(*s))
                    dve.wait_ge(sqrted.sem, sqrted.at(*s))
                    op(nc.vector.reciprocal(RS[:, :], SS[:, :]))
                    after()
                    if kind == "final":
                        dve.wait_ge(final_gain, 16)
                    for tt in range(2):
                        h, x, r = H[:, 2 * st + tt, :], X[:, 2 * st + tt, :], RS[:, tt:tt + 1]
                        if kind == "norm":
                            ins = nc.vector.tensor_scalar(h, x, r, None, ALU.mult)
                        else:
                            ins = nc.vector.scalar_tensor_tensor(out=h, in0=x, scalar=r, in1=G1B, op0=ALU.mult, op1=ALU.mult)
                        if tt == 0:
                            op(ins)
                    op(ins, normed.sem, normed.at(*s))
                elif kind == "rows":
                    _, l, st = s
                    dve.wait_ge(*evac(("bc", l, st, SH2, 1)))
                    dve.wait_ge(product, work[("hT", l, 2, st, KC // 2 - 1)] + 1)
                    after()
                    h = H[:, 2 * st:2 * st + 2, :]
                    op(nc.vector.tensor_tensor(h, h, A2B.unsqueeze(1).to_broadcast([P, 2, D]), ALU.mult))
                    after()
                    op(nc.vector.tensor_tensor(h, h, B2B.unsqueeze(1).to_broadcast([P, 2, D]), ALU.add),
                       modulated.sem, modulated.at(*s))
                elif kind == "rope":
                    l, tile = s[1], s[2]
                    st, tt = tile // 2, tile % 2
                    for b in (1, 2, 3, 4):
                        if st == LAT or (b == 4) == (s[3] == "k"):
                            dve.wait_ge(*evac(("in", l, b, st)))
                    after()
                    nh = {"qk": 16 if l == 0 else 20, "q": 12, "k": 4}[s[3]]
                    R = QKVL[:, tt, QOFF[l]:QOFF[l] + nh * HD] if st == LAT else QNC[:, tt, :] if s[3] == "q" else KN[:, tt, :]
                    R = R.rearrange("p (h n) -> p h n", n=HD)
                    a1 = T1[:, 0:nh * HD].rearrange("p (h n) -> p h n", n=HD)
                    a2 = T2[:, 0:nh * HD].rearrange("p (h n) -> p h n", n=HD)
                    if l == 0:
                        op(nc.vector.tensor_tensor(a1, R, R, ALU.mult))
                        after()
                        op(nc.vector.tensor_reduce(out=HS[:, 0:nh], in_=a1, axis=AX.X, op=ALU.add), hsumsq.sem, hsumsq.at(*s))
                        dve.wait_ge(hsqrt.sem, hsqrt.at(*s))
                        op(nc.vector.reciprocal(HR[:, 0:nh], HS[:, 0:nh]))
                        after()
                        op(nc.vector.tensor_tensor(R, R, HR[:, 0:nh].unsqueeze(2).to_broadcast([P, nh, HD]), ALU.mult))
                        after()
                        groups = {"qk": [(0, 12, 0), (12, 16, 1)], "q": [(0, 12, 0)], "k": [(0, 4, 1)]}[s[3]]
                    else:
                        groups = [(0, 20, None)]
                    if st == CTX:
                        (lo, hi, q), = groups
                        op(nc.vector.tensor_tensor(R, R, GN[:, q, :].unsqueeze(1).to_broadcast([P, nh, HD]), ALU.mult),
                           roped.sem, roped.at(*s))
                    else:
                        for lo, hi, q in groups:
                            tab = RC[:, tt, :, :] if q is None else CG[:, tt, q, :, :]
                            op(nc.vector.tensor_tensor(a1[:, lo:hi, :], R[:, lo:hi, :],
                                                       tab[:, 0, :].unsqueeze(1).to_broadcast([P, hi - lo, HD]), ALU.mult))
                            for a in range(2):
                                for half in range(2):
                                    o = 32 * half + 16 * a
                                    i = 32 * half + 16 * (1 - a)
                                    op(nc.vector.tensor_tensor(
                                        a2[:, lo:hi, o:o + 16], R[:, lo:hi, i:i + 16],
                                        tab[:, 1, o:o + 16].unsqueeze(1).to_broadcast([P, hi - lo, 16]), ALU.mult))
                        after()
                        op(nc.vector.tensor_tensor(R, a1, a2, ALU.add), roped.sem, roped.at(*s))
                elif kind == "att":
                    _, l, st, i0, n = s
                    us = units(l)

                    def rowmax(i):
                        name = s[:3] + ("A", i)
                        h = us[i][1]
                        ready(name)
                        m = STM[:, i % 4, :, :]
                        op(nc.vector.tensor_reduce(out=m[:, 0, :], in_=att_scores(name), axis=AX.X, op=ALU.max))
                        after()
                        if l == 0:
                            op(nc.vector.tensor_scalar(m[:, 1, :], m[:, 0, :], -SCALE, None, ALU.mult),
                               maxed.sem, maxed.at(l, st, i))
                        else:
                            sink = SK[:, h:h + 2]
                            op(nc.vector.scalar_tensor_tensor(out=m[:, 0, :], in0=m[:, 0, :], scalar=SCALE, in1=sink,
                                                              op0=ALU.mult, op1=ALU.max))
                            after()
                            op(nc.vector.tensor_tensor(m[:, 3, :], sink, m[:, 0, :], ALU.subtract))
                            op(nc.vector.tensor_scalar(m[:, 1, :], m[:, 0, :], -1.0, None, ALU.mult),
                               maxed.sem, maxed.at(l, st, i))

                    def rescale(i):
                        m = STM[:, i % 4, :, :]
                        dve.wait_ge(expd.sem, expd.at(l, st, i))
                        if l == 1:
                            op(nc.vector.tensor_tensor(m[:, 2, :], m[:, 2, :], m[:, 3, :], ALU.add))
                            after()
                        op(nc.vector.reciprocal(m[:, 2, :], m[:, 2, :]))
                        after()
                        for hh in range(2):
                            row = PR[st][:, i % 2, hh, :]
                            ins = nc.vector.tensor_scalar(row, row, m[:, 2, hh:hh + 1], None, ALU.mult)
                            if hh == 0:
                                op(ins)
                        op(ins, scaled.sem, scaled.at(l, st, i))

                    def values(i):
                        tt, h = us[i]
                        name = s[:3] + ("C", i)
                        ready(name)
                        taken(nc.vector.tensor_copy(YT[st][:, (2 if l == 0 else 0) + h // 2, tt * P:tt * P + P],
                                                    bank(name)[:, 0:P]), name)

                    rowmax(i0)
                    rowmax(i0 + 1)
                    rescale(i0)
                    for i in range(i0, n):
                        if i + 1 < n:
                            rescale(i + 1)
                        if i + 2 < n:
                            rowmax(i + 2)
                        if i > i0:
                            values(i - 1)
                    values(n - 1)
                elif kind == "out":
                    _, l, st = s
                    dve.wait_ge(*evac(("bc", l, st, G1, 1)))
                    for b in range(D // CW):
                        name = s + (b,)
                        ready(name)
                        y = bank(name).rearrange("p (a n) -> p a n", a=2)
                        g = G1B[:, b * CW:(b + 1) * CW].unsqueeze(1).to_broadcast([P, 2, CW])
                        x = X[:, 2 * st:2 * st + 2, b * CW:(b + 1) * CW]
                        op(nc.vector.tensor_tensor(y, y, g, ALU.mult))
                        after()
                        taken(nc.vector.tensor_tensor(x, x, y, ALU.add), name)
                elif kind == "topk":
                    _, l, tile, q = s
                    st, tt = tile // 2, tile % 2
                    dve.wait_ge(*evac(("score", l, st, "R", 2 * q + 1)))
                    after()
                    topk16([(TV[:, side, h, :], TI[:, side, h, :], SC[:, tt, 2 * (2 * q + h) + side, :])
                            for h in range(2) for side in range(2)])
                    op(nc.vector.tensor_scalar(TF[:, 0, :, :], TI[:, 0, :, :], float(NKEYS), float(l * NEXP), ALU.mult, ALU.add),
                       scores_used.sem, scores_used.at(*s))
                    op(nc.vector.tensor_copy(TF[:, 1, :, :], TI[:, 1, :, :]))
                    after()
                    for dst, src in ((CA, TV), (CI, TF)):
                        o = 0
                        for r0, nr, ncol in CAND:
                            out = dst[:, :, o:o + nr * ncol].rearrange("p h (a b) -> p h a b", a=nr)
                            first = src[:, 0, :, r0:r0 + nr].unsqueeze(3).to_broadcast([P, 2, nr, ncol])
                            second = src[:, 1, :, 0:ncol].unsqueeze(2).to_broadcast([P, 2, nr, ncol])
                            op(nc.vector.tensor_tensor(out, first, second, ALU.add))
                            o += nr * ncol
                    after()
                    topk16([(SV[:, h, :], PI[:, h, :], CA[:, h, :]) for h in range(2)])
                    op(nc.vector.tensor_copy(PF[:, :, :], PI[:, :, :]))
                    op(nc.vector.tensor_copy(SM[:, :], SV[:, :, 0]))
                    after()
                    op(nc.vector.tensor_tensor(SV[:, :, :], SV[:, :, :], SM[:, :].unsqueeze(2).to_broadcast([P, 2, TOPK]), ALU.subtract),
                       shifted.sem, shifted.at(*s))
                    k50 = [P, 2 * TOPK, NCAND]
                    op(nc.vector.tensor_tensor(OH3, PF[:, :, :].rearrange("p h k -> p (h k)").unsqueeze(2).to_broadcast(k50),
                                               IOF[:, :].unsqueeze(1).to_broadcast(k50), ALU.is_equal))
                    after()
                    op(nc.vector.tensor_tensor(OH, OH, CI[:, :, :].unsqueeze(2).to_broadcast([P, 2, TOPK, NCAND]), ALU.mult))
                    after()
                    op(nc.vector.tensor_reduce(out=IF[:, :, :].rearrange("p h k -> p (h k)"), in_=OH3, axis=AX.X, op=ALU.add))
                    dve.wait_ge(texp.sem, texp.at(*s))
                    op(nc.vector.tensor_reduce(out=SM[:, :], in_=SV[:, :, :], axis=AX.X, op=ALU.add))
                    after()
                    cols = slice(2 * q * TOPK, 2 * (q + 1) * TOPK)
                    op(nc.vector.tensor_copy(IDX[:, tile % 2, cols], IF[:, :, :].rearrange("p h k -> p (h k)")))
                    op(nc.vector.reciprocal(SM[:, :], SM[:, :]))
                    after()
                    op(nc.vector.tensor_tensor(WG[:, tile % 2, cols].rearrange("p (h k) -> p h k", k=TOPK), SV[:, :, :],
                                               SM[:, :].unsqueeze(2).to_broadcast([P, 2, TOPK]), ALU.mult),
                       chosen.sem, chosen.at(*s))
                elif kind == "experts":
                    _, l, tile, part = s
                    if part == "0":
                        after()
                        chunk(l, tile, 0, 0, tile - 1, tile == 0)
                        last[0] = (weighted, chunk0(l, tile) + 1) if tile == 0 else (updated, 2 * chunk0(l, tile))
                    elif part == "loop":
                        after()
                        with dve.Fori(1, PH // 2 - 1) as p:
                            chunk(l, tile, p, 0, tile, False)
                            chunk(l, tile, p, 1, tile, False)
                        last[0] = (updated, 2 * (chunk0(l, tile) + 5))
                    else:
                        h = int(part)
                        chunk(l, tile, h // 2, h % 2, tile, False)
                        last[0] = (updated, 2 * (chunk0(l, tile) + h))
                elif kind == "experts_end":
                    l = s[1]
                    tile = TILES[l][-1]
                    c = chunk0(l, tile) + PH - 1
                    update(c, 1, tile)
                    last[0] = (updated, 2 * c + 2)

        @block.scalar
        def _(act):
            def taken(ins, name):
                ins.then_inc(act_evac, 1)

            def ready(name):
                act.wait_ge(product, work[name] + 1)

            def gelu(c, hh):
                act.wait_ge(dotted, (c + 1) * TOPK)
                nc.scalar.activation(GA[:, hh, :], A[:, hh, :], ACT.Gelu).then_inc(gelud, 1)

            def diags(c, hh):
                act.wait_ge(weighted, c + 1)
                for s in range(TOPK):
                    if not (isinstance(c, int) and c == 0 and s < 4):
                        act.wait_ge(vsum, c * TOPK + s - 3)
                    nc.scalar.activation(DG[:, s % 4, :], ident[:, :], ACT.Copy, scale=WT[:, hh, s:s + 1]).then_inc(diag, 1)

            for s in SCHEDULE:
                kind = s[0]
                if kind == "prep":
                    ready(("rows",))
                    taken(nc.scalar.activation(CT[:, :], bank(("rows",))[:, 0:144], ACT.Copy), ("rows",))
                    act.wait_ge(act_evac, 1)
                    nc.scalar.activation(SE[:, :, :], CT[:, 0:16].rearrange("p (s j) -> p s j", s=2), ACT.Exp,
                                         scale=-1.0).then_inc(exp_c, 1)
                    ready(("keys",))
                    taken(nc.scalar.activation(KT[:, :, :].rearrange("p k n -> p (k n)"), bank(("keys",)), ACT.Copy), ("keys",))
                elif kind == "ada" and s[2] < HALVES:
                    ready(s)
                    taken(nc.scalar.activation(MROW[:, s[2] % 2, :], bank(s), ACT.Copy), s)
                elif kind in ("norm", "final"):
                    act.wait_ge(sumsq.sem, sumsq.at(*s))
                    nc.scalar.activation(SS[:, :], SS[:, :], ACT.Sqrt, bias=EPT[:, :], scale=1.0 / D).then_inc(sqrted.sem, 1)
                elif kind == "hT":
                    _, l, which, st = s
                    shift, scale = (SH1, SC1) if which == 1 else (SH2, SC2)
                    act.wait_ge(*evac(("adaT", l, 3 if which == 1 else HALVES - 1)))
                    for jj in range(KC // 2):
                        name = s + (jj,)
                        ready(name)
                        cols = slice(st * 256, st * 256 + 256)
                        for c in range(2):
                            j = 2 * jj + c
                            ins = nc.scalar.activation(HT[:, j, cols], bank(name)[:, c * 256:c * 256 + 256], ACT.Identity,
                                                       bias=MOD[:, l, shift * 8 + j, st:st + 1],
                                                       scale=MOD[:, l, scale * 8 + j, st:st + 1])
                        taken(ins, name)
                elif kind == "in":
                    _, l, b, streams = s
                    if s == ("in", 0, 1, (CTX,)):
                        act.wait_ge(scores_used.sem, scores_used.at("topk", 0, 0, 3))
                    for st in streams:
                        name = s[:3] + (st,)
                        ready(name)
                        dst = QKVL[:, :, b * CW:(b + 1) * CW] if st == LAT else \
                            {0: UN, 4: KN, 5: VC}[b][:, :, :] if b in (0, 4, 5) else QNC[:, :, (b - 1) * CW:b * CW]
                        taken(nc.scalar.activation(dst, bank(name).rearrange("p (a n) -> p a n", a=2), ACT.Copy), name)
                elif kind == "pool":
                    st = s[1]
                    for a, g in pool_steps():
                        name = s + (a, g)
                        ready(name)
                        if a == "PA":
                            taken(nc.scalar.activation(PL[0:64, g % 2, :], bank(name)[0:64, 0:256], ACT.Copy), name)
                        else:
                            o = 64 * (g % 2)
                            taken(nc.scalar.activation(YT[st][o:o + 64, g // 2, :], bank(name)[o:o + 64, 0:256], ACT.Copy,
                                                       scale=PS[o:o + 64, g // 2:g // 2 + 1]), name)
                elif kind == "rope" and s[1] == 0:
                    act.wait_ge(hsumsq.sem, hsumsq.at(*s))
                    nh = {"qk": 16, "q": 12, "k": 4}[s[3]]
                    nc.scalar.activation(HS[:, 0:nh], HS[:, 0:nh], ACT.Sqrt, bias=EPT[:, :], scale=1.0 / HD).then_inc(hsqrt.sem, 1)
                elif kind == "tqk":
                    dst = (QT if s[3] == "q" else KTS)[s[2]]
                    for name, _ in WORK:
                        if name[:4] == s:
                            ready(name)
                            i = name[4]
                            taken(nc.scalar.activation(dst[:, 2 * i:2 * i + 2, :],
                                                       bank(name).rearrange("p (c n) -> p c n", c=2), ACT.Copy), name)
                elif kind == "att":
                    _, l, st, i0, n = s
                    us = units(l)

                    def exps(i):
                        name = s[:3] + ("A", i)
                        m = STM[:, i % 4, :, :]
                        act.wait_ge(maxed.sem, maxed.at(l, st, i))
                        if l == 1:
                            nc.scalar.activation(m[:, 3, :], m[:, 3, :], ACT.Exp).then_inc(ach, 1)
                        for hh in range(2):
                            ins = nc.scalar.activation(PR[st][:, i % 2, hh, :], att_scores(name)[:, hh, :], ACT.Exp,
                                                       bias=m[:, 1, hh:hh + 1], scale=SCALE, accum_out=m[:, 2, hh:hh + 1])
                        ins.then_inc(expd.sem, 1)

                    exps(i0)
                    exps(i0 + 1)
                    for i in range(i0, n):
                        name = s[:3] + ("B", i)
                        ready(name)
                        taken(nc.scalar.activation(PT[st][:, i % 2, :, :], att_turned(name), ACT.Copy), name)
                        if i + 2 < n:
                            exps(i + 2)
                elif kind == "bc":
                    _, l, st, vectors = s
                    if (l, st) != (0, LAT):
                        act.wait_ge(modulated.sem, modulated.at("rows", 0, LAT if l == 0 else CTX))
                    for v in vectors:
                        dst = {G1: G1B, SC2: A2B, SH2: B2B, G2: G2B[st]}[v]
                        for hf in range(2):
                            name = s[:3] + (v, hf)
                            ready(name)
                            taken(nc.scalar.activation(dst[:, hf * 512:hf * 512 + 512], bank(name), ACT.Copy), name)
                elif kind == "score":
                    _, l, st, heads = s
                    for a, h in score_steps(heads):
                        name = ("score", l, st, a, h)
                        ready(name)
                        if a == "Q":
                            taken(nc.scalar.activation(QS[:, h % 2, :, :], bank(name).rearrange("p (a n) -> p a n", a=2),
                                                       ACT.Copy), name)
                        else:
                            if st == CTX:
                                act.wait_ge(scores_used.sem, scores_used.at("topk", l, 1, h // 2))
                            taken(nc.scalar.activation(SC[:, :, 2 * h:2 * h + 2, :],
                                                       bank(name).rearrange("p (a s n) -> p a s n", a=2, s=2), ACT.Copy), name)
                elif kind == "topk":
                    act.wait_ge(shifted.sem, shifted.at(*s))
                    nc.scalar.activation(SV[:, :, :], SV[:, :, :], ACT.Exp).then_inc(texp.sem, 1)
                elif kind == "experts":
                    _, l, tile, part = s
                    c0 = chunk0(l, tile)
                    if part != "loop":
                        c = c0 + int(part)
                        if c > chunk0(l, 0):
                            diags(c - 1, (c - 1) % 2)
                        gelu(c, c % 2)
                    else:
                        with act.Fori(1, PH // 2 - 1) as p:
                            diags(c0 + 2 * p - 1, 1)
                            gelu(c0 + 2 * p, 0)
                            diags(c0 + 2 * p, 0)
                            gelu(c0 + 2 * p + 1, 1)
                elif kind == "experts_end":
                    diags(chunk0(s[1], TILES[s[1]][-1]) + PH - 1, 1)

        @block.tensor
        def _(pe):
            n_work = [0]

            def begin(name):
                i = work[name]
                assert i == n_work[0], (name, WORK[n_work[0]])
                n_work[0] += 1
                for b in BEFORE[name]:
                    pe.wait_ge(*evac(b))
                return bank(name) if BANKS[name] else None

            def done(ins):
                ins.then_inc(product, 1)

            def weights(name):
                slot, count, _ = SLOTS[blk[name]]
                pe.wait_ge(blk_in[slot], 16 * count)
                return slot_rows(slot)

            def tr(out, in_, k=P):
                return nc.tensor.transpose(out, in_, ident[0:k, 0:k])

            def vsums(c, par):
                if not (isinstance(c, int) and c < 2):
                    pe.wait_ge(updated, 2 * c - 2)
                for s in range(TOPK):
                    pe.wait_ge(v_in[s % NV], 16 * (2 * c + s // NV + 1))
                    pe.wait_ge(diag, c * TOPK + s + 1)
                    for hf in range(2):
                        ins = nc.tensor.matmul(acc[:, par, hf * 512:hf * 512 + 512], DG[:, s % 4, :],
                                               V[:, s % NV, hf * 512:hf * 512 + 512],
                                               start=(s == 0), stop=(s == TOPK - 1))
                    ins.then_inc(vsum, 1)

            for s in SCHEDULE:
                kind = s[0]
                if kind == "prep":
                    pe.wait_ge(consts, 6)
                    pe.wait_ge(loaded["rows"], 96)
                    o = begin(("rows",))
                    tr(o[:, 0:96], R1[:, :], 96)
                    done(tr(o[:, 96:144], R2[:, :], 48))
                    pe.wait_ge(loaded["keys"], 64)
                    o = begin(("keys",))
                    for k in range(4):
                        ins = tr(o[:, k * P:k * P + P], KR[:, k, :])
                    done(ins)
                elif kind == "ada":
                    _, l, k = s
                    if k < HALVES:
                        if k == 0:
                            pe.wait_ge(silu_done, 1)
                        o = begin(s)
                        for b in range(2):
                            w = weights(("ada", l, 2 * k + b))
                            for j in range(KC):
                                g = 32 * (j % 4)
                                ins = nc.tensor.matmul(o[g:g + 32, b * CW:(b + 1) * CW], SIL[:, j, :], w[:, j, :],
                                                       start=(j < 4), stop=(j >= 4))
                            if b == 0:
                                ins.then_inc(ada_first, 1)
                        done(ins)
                    if k > 0:
                        name = ("adaT", l, k - 1)
                        pe.wait_ge(*evac(("ada", l, k - 1)))
                        o = begin(name)
                        for i in range(4):
                            ins = nc.tensor.matmul(o[:, 2 * i:2 * i + 2], MROW[:, (k - 1) % 2, i * P:i * P + P], SEL[:, :],
                                                   start=True, stop=True)
                        done(ins)
                elif kind == "hT":
                    _, l, which, st = s
                    pe.wait_ge(normed.sem, normed.at("norm", l, which, st))
                    for jj in range(KC // 2):
                        o = begin(s + (jj,))
                        for c in range(2):
                            for tt in range(2):
                                ins = tr(o[:, c * 256 + tt * P:c * 256 + tt * P + P],
                                         H[:, 2 * st + tt, (2 * jj + c) * P:(2 * jj + c + 1) * P])
                        done(ins)
                elif kind == "in":
                    _, l, b, streams = s
                    w = weights(s)
                    for st in streams:
                        pe.wait_ge(*evac(("hT", l, 1, st, KC // 2 - 1)))
                        o = begin(s[:3] + (st,))
                        for tt in range(2):
                            for j in range(KC):
                                ins = nc.tensor.matmul(o[:, tt * CW:(tt + 1) * CW],
                                                       HT[:, j, (2 * st + tt) * P:(2 * st + tt + 1) * P], w[:, j, :],
                                                       start=(j == 0), stop=(j == KC - 1))
                        done(ins)
                elif kind == "tqk":
                    _, l, st, part = s
                    for r_ in ropes:
                        if r_[1] == l and r_[2] // 2 == st and part in r_[3]:
                            pe.wait_ge(roped.sem, roped.at(*r_))
                    if (l, st) == (1, CTX):
                        pe.wait_ge(*evac(("in", l, 4, st)))
                    for name, _ in WORK:
                        if name[:4] == s:
                            o = begin(name)
                            for c in range(2):
                                for tt in range(2):
                                    i = 2 * name[4] + c
                                    cols = slice(c * 256 + tt * P, c * 256 + tt * P + P)
                                    if part == "q":
                                        src = QKVL[:, tt, QOFF[l] + i * P:QOFF[l] + (i + 1) * P] if st == LAT else \
                                            QNC[:, tt, i * P:(i + 1) * P]
                                        ins = tr(o[:, cols], src)
                                    else:
                                        src = QKVL[:, tt, KOFF + i * HD:KOFF + (i + 1) * HD] if st == LAT else \
                                            KN[:, tt, i * HD:(i + 1) * HD]
                                        for q0 in (0, 64):
                                            ins = nc.tensor.matmul(o[q0:q0 + 64, cols], src, ident[:, :],
                                                                   start=True, stop=True)
                            done(ins)
                elif kind == "att":
                    _, l, st, i0, n = s
                    us = units(l)
                    group = QH[l] // NKV
                    pe.wait_ge(*evac(("tqk", l, st, "q", QH[l] // 4 - 1)))
                    for stk in (LAT, CTX):
                        pe.wait_ge(*evac(("tqk", l, stk, "k", 1)))
                    pe.wait_ge(*evac(("in", l, 5, CTX)))
                    for a, i in att_steps(i0, n):
                        tt, h = us[i]
                        name = s[:3] + (a, i)
                        if a == "A":
                            begin(name)
                            if i >= i0 + 2:
                                pe.wait_ge(*evac(s[:3] + ("A", i - 2)))
                            o = att_scores(name)
                            for k0, stk in (((256, CTX), (0, LAT)) if st == LAT else ((0, CTX),)):
                                for hh in range(2):
                                    q0 = 64 * hh
                                    ins = nc.tensor.matmul(o[:, hh, k0:k0 + 256], QT[st][q0:q0 + 64, h // 2, tt * P:tt * P + P],
                                                           KTS[stk][q0:q0 + 64, (h + hh) // group, :], start=True,
                                                           stop=not (l == 1 and stk == LAT))
                            if l == 1:
                                m0 = P * (1 - tt)
                                for hh in range(2):
                                    ins = nc.tensor.matmul(o[:, hh, m0:m0 + P], ident[:, :], MK[:, tt, :], start=False, stop=True)
                        elif a == "B":
                            pe.wait_ge(scaled.sem, scaled.at(l, st, i))
                            begin(name)
                            o = att_turned(name)
                            for hh in range(2):
                                for kc in range(4 if st == LAT else 2):
                                    ins = tr(o[:, hh, kc * P:kc * P + P], PR[st][:, i % 2, hh, kc * P:kc * P + P])
                        else:
                            pe.wait_ge(*evac(s[:3] + ("B", i)))
                            o = begin(name)
                            nkc = 4 if st == LAT else 2
                            for kc in range(nkc):
                                for hh in range(2):
                                    q0 = 64 * hh
                                    kv = (h + hh) // group
                                    v = QKVL[:, kc, VOFF + kv * HD:VOFF + (kv + 1) * HD] if st == LAT and kc < 2 else \
                                        VC[:, kc % 2, kv * HD:(kv + 1) * HD]
                                    ins = nc.tensor.matmul(o[q0:q0 + 64, 0:P], v, PT[st][:, i % 2, hh, kc * P:kc * P + P],
                                                           start=(kc == 0), stop=(kc == nkc - 1))
                        done(ins)
                elif kind == "pool":
                    st = s[1]
                    pe.wait_ge(loaded["pm"], 16)
                    pe.wait_ge(loaded["small"], 96)
                    pe.wait_ge(*evac(("in", 0, 0, st)))
                    for a, g in pool_steps():
                        name = s + (a, g)
                        if a == "PA":
                            o = begin(name)
                            for tt in range(2):
                                un = (QKVL if st == LAT else UN)[:, tt, g * 64:g * 64 + 64]
                                ins = nc.tensor.matmul(o[0:64, 0:256], un, PM[:, tt, g, :],
                                                       start=(tt == 0), stop=(tt == 1))
                        else:
                            pe.wait_ge(*evac(s + ("PA", g)))
                            o = begin(name)
                            q0 = 64 * (g % 2)
                            ins = nc.tensor.matmul(o[q0:q0 + 64, 0:256], PW[:, g, :], PL[0:64, g % 2, :], start=True, stop=True)
                        done(ins)
                elif kind == "bc":
                    _, l, st, vectors = s
                    pe.wait_ge(*evac(("adaT", l, HALVES - 1)))
                    for v in vectors:
                        for hf in range(2):
                            o = begin(s[:3] + (v, hf))
                            for i in range(4):
                                j = 4 * hf + i
                                ins = nc.tensor.matmul(o[:, i * P:i * P + P],
                                                       MOD[:, l, v * 8 + j, st:st + 1].to_broadcast([P, P]), ident[:, :],
                                                       start=True, stop=True)
                            done(ins)
                elif kind == "out":
                    _, l, st = s
                    pe.wait_ge(*evac(("att", l, st, "C", len(units(l)) - 1)))
                    if l == 0:
                        pe.wait_ge(*evac(("pool", st, "PB", 3)))
                    for b in range(D // CW):
                        w = weights(s + (b,))
                        o = begin(s + (b,))
                        for tt in range(2):
                            for j in range(KC):
                                ins = nc.tensor.matmul(o[:, tt * CW:(tt + 1) * CW], YT[st][:, j, tt * P:tt * P + P], w[:, j, :],
                                                       start=(j == 0), stop=(j == KC - 1))
                        done(ins)
                elif kind == "score":
                    _, l, st, heads = s
                    pe.wait_ge(*evac(("hT", l, 2, st, KC // 2 - 1)))
                    for a, h in score_steps(heads):
                        name = ("score", l, st, a, h)
                        if a == "Q":
                            w = weights(("wq", l, st, h))
                            o = begin(name)
                            for half in range(2):
                                for j in range(KC):
                                    ins = nc.tensor.matmul(o[:, half * 256:half * 256 + 256], w[:, j, half * P:half * P + P],
                                                           HT[:, j, st * 256:st * 256 + 256], start=(j == 0), stop=(j == KC - 1))
                            done(ins)
                        else:
                            pe.wait_ge(*evac(("score", l, st, "Q", h)))
                            o = begin(name)
                            for tt in range(2):
                                for half in range(2):
                                    ins = nc.tensor.matmul(o[:, (2 * tt + half) * P:(2 * tt + half + 1) * P],
                                                           QS[:, h % 2, half, tt * P:tt * P + P], KT[:, 2 * l + half, :],
                                                           start=True, stop=True)
                            done(ins)
                elif kind == "experts":
                    _, l, tile, part = s
                    c0 = chunk0(l, tile)
                    if part != "loop":
                        c = c0 + int(part)
                        if c > chunk0(l, 0):
                            vsums(c - 1, (c - 1) % 2)
                    else:
                        with pe.Fori(1, PH // 2 - 1) as p:
                            vsums(c0 + 2 * p - 1, 1)
                            vsums(c0 + 2 * p, 0)
                elif kind == "experts_end":
                    vsums(chunk0(s[1], TILES[s[1]][-1]) + PH - 1, 1)


INPUTS = ["x", "c", "ctx", "c_ctx", "ada_w", "ada_b", "norm1_g", "norm2_g", "final_g", "e_w_in", "e_q_norm_g",
          "e_k_norm_g", "e_pool_w", "e_pool_scale", "e_w_out", "o_w_in", "o_sink", "o_w_out", "p_w_q", "p_keys1",
          "p_keys2", "p_u", "p_v"]


def shape_constants(seq, head_dim):
    import numpy as np
    grid_w, half = 64, head_dim // 2
    pos = np.arange(seq)
    inv = (1.0 / (np.float32(10000.0) ** (np.arange(0, half, 2, dtype=np.float32) / np.float32(half)))).astype(np.float32)
    rope = np.zeros((2, 128, 2, head_dim), np.float32)
    for axis, coord in enumerate((pos // grid_w, pos % grid_w)):
        ang = coord.astype(np.float32)[:, None] * inv[None, :]
        cos, sin = np.cos(ang).astype(np.float32), np.sin(ang).astype(np.float32)
        o = axis * half
        c = np.concatenate([cos, cos], 1).reshape(2, 128, half)
        s = np.concatenate([-sin, sin], 1).reshape(2, 128, half)
        rope[:, :, 0, o:o + half] = c
        rope[:, :, 1, o:o + half] = s
    pm = np.zeros((4, seq, seq), np.float32)
    for g, w in enumerate((2, 4, 8, 16)):
        for q in range(seq):
            lo, hi = max(q - w // 2, 0), min(q + w - w // 2, seq)
            pm[g, lo:hi, q] = np.float32(1.0) / np.float32(hi - lo)
            pm[g, q, q] -= 1.0
    pool = pm.reshape(4, 2, 128, seq).transpose(2, 1, 0, 3)
    return np.ascontiguousarray(rope.transpose(1, 0, 2, 3)), np.ascontiguousarray(pool)


def kernel(**inputs):
    import numpy as np
    import concourse.bacc as bacc
    from concourse.bass_utils import run_bass_kernel_spmd as run

    nc = bacc.Bacc("TRN2", target_bir_lowering=False, num_devices=1)
    arrays, tensors = {}, {}
    rope, pool_m = shape_constants(256, 64)
    for name in INPUTS + ["rope", "pool_m"]:
        a = {"rope": rope, "pool_m": pool_m}[name] if name in ("rope", "pool_m") else np.ascontiguousarray(inputs[name])
        arrays[f"in_{name}"] = a
        tensors[name] = nc.dram_tensor(f"in_{name}", a.shape, mybir.dt.from_np(a.dtype), kind="ExternalInput").ap()
    tensors["out"] = nc.dram_tensor("out_x", (1, 256, 1024), F32, kind="ExternalOutput").ap()
    program(nc, tensors)
    r = run(nc, [arrays], core_ids=[0])
    return r.results[0]["out_x"]
```
